# Optimizing a Trainium2 kernel written in Bass

```python
import jax, jax.numpy as jnp
from jax import lax
import numpy as np

D_MODEL = 1024
BATCH = 1
SEQ = 512
DEPTH = 1
DEC_BATCH = 8
DEC_SEQ = 4
PAST_LEN = 256
PAGE_SIZE = 128

HEAD_DIM = 64
N_HEADS = 12
ATTN_WIDTH = N_HEADS * HEAD_DIM
CONV_CH = D_MODEL - ATTN_WIDTH
CONV_GROUPS = CONV_CH // HEAD_DIM
CONV_WIDTH = 31
IN_COLS = 3 * ATTN_WIDTH + 2 * CONV_CH
DILATIONS = ((128, 1), (512, 4), (2048, 16))
MAX_WINDOW = 2048
BAND_BLOCK = 128
ROPE_THETA = 10000.0
ATTN_SCALE = HEAD_DIM ** -0.5
NEG_INF = -1e30
N_KEYS = 128
N_EXPERTS = N_KEYS * N_KEYS
PEER_HEADS = 8
PEER_TOPK = 16
D_QUERY = 256
HALF_Q = D_QUERY // 2
PEER_CHUNK = 256
RMS_EPS = 1e-6
LN_EPS = 1e-5

kernel_name = 'hymba_conformer_dilated_peer_step'

def rms_norm(x, g):
    xf = x.astype(jnp.float32)
    y = xf * lax.rsqrt(jnp.mean(xf * xf, axis=-1, keepdims=True) + RMS_EPS)
    return (y * g.astype(jnp.float32)).astype(x.dtype)

def rope(x, pos):
    half = HEAD_DIM // 2
    inv = jnp.power(ROPE_THETA, -jnp.arange(half, dtype=jnp.float32) * (2.0 / HEAD_DIM))
    ang = pos.astype(jnp.float32)[:, None] * inv[None, :]
    cos = jnp.cos(ang)[None, :, None, :]
    sin = jnp.sin(ang)[None, :, None, :]
    xf = x.astype(jnp.float32)
    x1, x2 = xf[..., :half], xf[..., half:]
    return jnp.concatenate([x1 * cos - x2 * sin, x2 * cos + x1 * sin], axis=-1).astype(x.dtype)

def in_projection(h, w_in):
    p = h @ w_in
    lead = p.shape[:-1]
    q = p[..., :ATTN_WIDTH].reshape(lead + (N_HEADS, HEAD_DIM))
    k = p[..., ATTN_WIDTH:2 * ATTN_WIDTH].reshape(lead + (N_HEADS, HEAD_DIM))
    v = p[..., 2 * ATTN_WIDTH:3 * ATTN_WIDTH].reshape(lead + (N_HEADS, HEAD_DIM))
    u = p[..., 3 * ATTN_WIDTH:]
    g = u[..., :CONV_CH] * jax.nn.sigmoid(u[..., CONV_CH:])
    return q, k, v, g

def banded_branch(q, k, v, dil, reach):
    b, s, h, dh = q.shape
    L = s // dil
    n = b * dil
    Q = BAND_BLOCK
    nb = -(-L // Q)
    lp = nb * Q

    def to_sub(t):
        return t.reshape(b, L, dil, h, dh).transpose(0, 2, 1, 3, 4).reshape(n, L, h, dh)

    qs = jnp.pad(to_sub(q), ((0, 0), (0, lp - L), (0, 0), (0, 0))).reshape(n, nb, Q, h, dh)

    def key_blocks(t):
        t = jnp.pad(to_sub(t), ((0, 0), (Q, lp - L), (0, 0), (0, 0))).reshape(n, nb + 1, Q, h, dh)
        return jnp.concatenate([t[:, :-1], t[:, 1:]], axis=2)

    kb = key_blocks(k)
    vb = key_blocks(v)
    qi = jnp.arange(Q)[:, None]
    ki = jnp.arange(2 * Q)[None, :]
    dist = qi + Q - ki
    blk = jnp.arange(nb)[:, None, None]
    valid = (dist >= 0) & (dist <= reach) & (blk * Q - Q + ki >= 0)
    sc = jnp.einsum('nbqhd,nbkhd->nbhqk', qs, kb, preferred_element_type=jnp.float32) * ATTN_SCALE
    sc = jnp.where(valid[None, :, None], sc, NEG_INF)
    m = sc.max(axis=-1)
    p = jnp.exp(sc - m[..., None])
    l = p.sum(axis=-1)
    o = jnp.einsum('nbhqk,nbkhd->nbqhd', p, vb.astype(jnp.float32))

    def from_sub(t):
        t = t.reshape((n, lp) + t.shape[3:])[:, :L]
        t = jnp.swapaxes(t.reshape((b, dil, L) + t.shape[2:]), 1, 2)
        return t.reshape((b, s) + t.shape[3:])

    return from_sub(o), from_sub(jnp.swapaxes(m, 2, 3)), from_sub(jnp.swapaxes(l, 2, 3))

def gathered_branch(q, k_all, v_all, offset, dil, reach):
    t = q.shape[1]
    idx = offset + jnp.arange(t)[:, None] - dil * jnp.arange(reach + 1)[None, :]
    valid = idx >= 0
    idx = jnp.maximum(idx, 0)
    kg = k_all[:, idx]
    vg = v_all[:, idx]
    sc = jnp.einsum('bthd,btrhd->bthr', q, kg, preferred_element_type=jnp.float32) * ATTN_SCALE
    sc = jnp.where(valid[None, :, None, :], sc, NEG_INF)
    m = sc.max(axis=-1)
    p = jnp.exp(sc - m[..., None])
    l = p.sum(axis=-1)
    o = jnp.einsum('bthr,btrhd->bthd', p, vg.astype(jnp.float32))
    return o, m, l

def merge_branches(parts):
    m_all = jnp.stack([pm for _, pm, _ in parts])
    l_all = jnp.stack([pl for _, _, pl in parts])
    o_all = jnp.stack([po for po, _, _ in parts])
    w = jnp.exp(m_all - m_all.max(axis=0))
    den = (w * l_all).sum(axis=0)
    out = (w[..., None] * o_all).sum(axis=0) / den[..., None]
    return out.reshape(out.shape[:2] + (ATTN_WIDTH,))

def conformer_conv(g_hist, conv_w, conv_b, ln_g, ln_b):
    y = lax.conv_general_dilated(g_hist, conv_w[:, None, :].astype(g_hist.dtype), (1,), 'VALID',
                                 dimension_numbers=('NWC', 'WIO', 'NWC'),
                                 feature_group_count=CONV_CH)
    yf = (y + conv_b).astype(jnp.float32)
    mu = jnp.mean(yf, axis=-1, keepdims=True)
    var = jnp.mean(jnp.square(yf - mu), axis=-1, keepdims=True)
    yn = (yf - mu) * lax.rsqrt(var + LN_EPS) * ln_g.astype(jnp.float32) + ln_b.astype(jnp.float32)
    return (yn * jax.nn.sigmoid(yn)).astype(g_hist.dtype)

def peer(x, w_query, keys1, keys2, exp_u, exp_v):
    T, D = x.shape
    nc = -(-T // PEER_CHUNK)
    xs = jnp.pad(x, ((0, nc * PEER_CHUNK - T), (0, 0))).reshape(nc, PEER_CHUNK, D)
    k1 = keys1.astype(jnp.float32)
    k2 = keys2.astype(jnp.float32)

    def chunk_fn(xc):
        q = (xc @ w_query).astype(jnp.float32).reshape(PEER_CHUNK, PEER_HEADS, D_QUERY)
        s1 = jnp.einsum('chk,nk->chn', q[..., :HALF_Q], k1)
        s2 = jnp.einsum('chk,nk->chn', q[..., HALF_Q:], k2)
        v1, i1 = lax.top_k(s1, PEER_TOPK)
        v2, i2 = lax.top_k(s2, PEER_TOPK)
        cand = (v1[..., :, None] + v2[..., None, :]).reshape(PEER_CHUNK, PEER_HEADS, PEER_TOPK * PEER_TOPK)
        sc, ci = lax.top_k(cand, PEER_TOPK)
        e1 = jnp.take_along_axis(i1, ci // PEER_TOPK, axis=-1)
        e2 = jnp.take_along_axis(i2, ci % PEER_TOPK, axis=-1)
        eid = e1 * N_KEYS + e2
        gate = jax.nn.softmax(sc, axis=-1)
        act = jax.nn.gelu(jnp.einsum('chkd,cd->chk', exp_u[eid], xc, preferred_element_type=jnp.float32))
        out = jnp.einsum('chk,chkd->cd', gate * act, exp_v[eid].astype(jnp.float32))
        return out.astype(xc.dtype)

    return lax.map(chunk_fn, xs).reshape(nc * PEER_CHUNK, D)[:T]

def channel_block(x, g, w_query, keys1, keys2, exp_u, exp_v):
    h = rms_norm(x, g)
    y = peer(h.reshape(-1, D_MODEL), w_query, keys1, keys2, exp_u, exp_v)
    return x + y.reshape(x.shape)

def setup_inputs(seed: int = 0) -> dict:
    key = jax.random.key(seed)
    ks = jax.random.split(key, 20)
    w_buf = min(MAX_WINDOW, PAST_LEN)

    def nrm(k, shape, s):
        return s * jax.random.normal(k, shape, jnp.float32)

    return {
        'x_prompt': nrm(ks[0], (BATCH, SEQ, D_MODEL), 1.0),
        'x_sample': nrm(ks[1], (DEC_BATCH, DEC_SEQ, D_MODEL), 1.0),
        'cache_k': nrm(ks[2], (DEPTH, DEC_BATCH, w_buf, N_HEADS, HEAD_DIM), 1.0),
        'cache_v': nrm(ks[3], (DEPTH, DEC_BATCH, w_buf, N_HEADS, HEAD_DIM), 1.0),
        'state_conv': nrm(ks[4], (DEPTH, DEC_BATCH, CONV_WIDTH - 1, CONV_CH), 0.5),
        'norm1_g': 1.0 + nrm(ks[5], (DEPTH, D_MODEL), 0.01),
        'w_in': nrm(ks[6], (DEPTH, D_MODEL, IN_COLS), D_MODEL ** -0.5),
        'conv_w': nrm(ks[7], (DEPTH, CONV_WIDTH, CONV_CH), CONV_WIDTH ** -0.5),
        'conv_b': nrm(ks[8], (DEPTH, CONV_CH), 0.01),
        'conv_ln_g': 1.0 + nrm(ks[9], (DEPTH, CONV_CH), 0.01),
        'conv_ln_b': nrm(ks[10], (DEPTH, CONV_CH), 0.01),
        'w_out': nrm(ks[11], (DEPTH, D_MODEL, D_MODEL), D_MODEL ** -0.5),
        'norm2_g': 1.0 + nrm(ks[12], (DEPTH, D_MODEL), 0.01),
        'w_query': nrm(ks[13], (DEPTH, D_MODEL, PEER_HEADS * D_QUERY), D_MODEL ** -0.5),
        'sub_keys1': nrm(ks[14], (DEPTH, N_KEYS, HALF_Q), HALF_Q ** -0.5),
        'sub_keys2': nrm(ks[15], (DEPTH, N_KEYS, HALF_Q), HALF_Q ** -0.5),
        'expert_u': nrm(ks[16], (DEPTH, N_EXPERTS, D_MODEL), D_MODEL ** -0.5),
        'expert_v': nrm(ks[17], (DEPTH, N_EXPERTS, D_MODEL), 0.5),
        'final_g': 1.0 + nrm(ks[18], (D_MODEL,), 0.01),
    }

def reference(x_prompt, x_sample, cache_k, cache_v, state_conv, norm1_g, w_in, conv_w, conv_b,
              conv_ln_g, conv_ln_b, w_out, norm2_g, w_query, sub_keys1, sub_keys2,
              expert_u, expert_v, final_g):
    bp, s = x_prompt.shape[:2]
    t = x_sample.shape[1]
    w_buf = cache_k.shape[2]
    keep = min(MAX_WINDOW, s)
    pos_p = jnp.arange(s)
    pos_s = PAST_LEN + jnp.arange(t)
    yp, ys = x_prompt, x_sample
    nkp, nvp, ncp, nks, nvs, ncs = [], [], [], [], [], []
    for l in range(DEPTH):
        q, k, v, g = in_projection(rms_norm(yp, norm1_g[l]), w_in[l])
        q = rope(q, pos_p)
        k = rope(k, pos_p)
        attn = merge_branches([banded_branch(q, k, v, dil, win // dil) for win, dil in DILATIONS])
        g_hist = jnp.concatenate([jnp.zeros((bp, CONV_WIDTH - 1, CONV_CH), g.dtype), g], axis=1)
        c = conformer_conv(g_hist, conv_w[l], conv_b[l], conv_ln_g[l], conv_ln_b[l])
        yp = yp + jnp.concatenate([attn.astype(yp.dtype), c], axis=-1) @ w_out[l]
        yp = channel_block(yp, norm2_g[l], w_query[l], sub_keys1[l], sub_keys2[l], expert_u[l], expert_v[l])
        nkp.append(k[:, s - keep:])
        nvp.append(v[:, s - keep:])
        ncp.append(g_hist[:, -(CONV_WIDTH - 1):])
        q, k, v, g = in_projection(rms_norm(ys, norm1_g[l]), w_in[l])
        q = rope(q, pos_s)
        k = rope(k, pos_s)
        k_all = jnp.concatenate([cache_k[l], k], axis=1)
        v_all = jnp.concatenate([cache_v[l], v], axis=1)
        attn = merge_branches([gathered_branch(q, k_all, v_all, w_buf, dil, win // dil)
                               for win, dil in DILATIONS])
        g_hist = jnp.concatenate([state_conv[l], g], axis=1)
        c = conformer_conv(g_hist, conv_w[l], conv_b[l], conv_ln_g[l], conv_ln_b[l])
        ys = ys + jnp.concatenate([attn.astype(ys.dtype), c], axis=-1) @ w_out[l]
        ys = channel_block(ys, norm2_g[l], w_query[l], sub_keys1[l], sub_keys2[l], expert_u[l], expert_v[l])
        nks.append(k)
        nvs.append(v)
        ncs.append(g_hist[:, -(CONV_WIDTH - 1):])
    y_prompt = rms_norm(yp, final_g)
    y_sample = rms_norm(ys, final_g)
    return (y_prompt, y_sample, jnp.stack(nkp), jnp.stack(nvp), jnp.stack(ncp),
            jnp.stack(nks), jnp.stack(nvs), jnp.stack(ncs))


_drawn_inputs = setup_inputs


def setup_inputs(seed=0):
    import zlib

    import numpy as np

    out = dict(_drawn_inputs(seed))
    spreads = {}
    factors = {'norm1_g': 3.192,
     'conv_ln_g': 71.48,
     'conv_ln_b': 69.843,
     'final_g': 190.852,
     'conv_b': 4.051,
     'norm2_g': 22.762}
    for name, (base, spread) in spreads.items():
        noise = np.random.default_rng([zlib.crc32(name.encode()), seed]).standard_normal(out[name].shape)
        drawn = base * np.exp(spread * noise) if base else spread * noise
        out[name] = __import__('jax').numpy.asarray(drawn.astype(out[name].dtype))
    for name, factor in factors.items():
        out[name] = (out[name] * factor).astype(out[name].dtype)
    return out
```

```python
from contextlib import ExitStack

import numpy as np

import concourse.bass as bass
from concourse import mybir

F32 = mybir.dt.float32
F32R = mybir.dt.float32r
BF16 = mybir.dt.bfloat16
U32 = mybir.dt.uint32
ALU = mybir.AluOpType
ACT = mybir.ActivationFunctionType
AX_X = mybir.AxisListType.X

P = 128
D = 1024
KT = D // P
SEQ = 512
DEC_B, DEC_T = 8, 4
NS = DEC_B * DEC_T
T = SEQ + NS
HT = T // 2
TILES = 5
ROWS = [P] * 4 + [NS]
HD, NH = 64, 12
AW = NH * HD
PAIRS = NH // 2
CH = D - AW
TAPS = 31
PAST = 256
CB = 256
NCB = (3 * AW + 2 * CH) // CB
NSK = PAST + NS
SROWS = NH * DEC_T
NEG = -1.0e30
SCALE = HD ** -0.5
RMS_EPS, LN_EPS = 1e-6, 1e-5
DILATIONS = ((128, 1), (512, 4), (2048, 16))
PH, TOPK, NK = 8, 16, 128
SLOTS = PH * TOPK
CPP = 16
PARTS = NK // CPP
CG = 4
GROUPS = CPP // CG
NG = PARTS * GROUPS
TB = 8
BPP = T // TB
UNITS = ((4, 4), (5, 5, 5, 5), (5, 5, 5, 5), (5, 5, 5, 5))
UPP = sum(len(g) for g in UNITS)
UT_MAX = max(max(g) for g in UNITS) * TB
HOTS = 4
LEAD = 2
VS = 4
VC = D // VS
assert sum(map(sum, UNITS)) == BPP and UPP % 2 == 0 and BPP % HOTS == 0


def group_steps(gg, build, weigh, last=False):
    heavy = []
    for c in range(CG):
        if not (last and c == CG - 1):
            heavy.append(("u", c + 1))
        heavy.append(("a", c, 0))
        if c or weigh:
            heavy.append(("p", c - 1, 1))
        heavy += [("a", c, 1), ("p", c, 0)]
        if weigh:
            lo, hi = (c, c + 1) if gg else (2 * c, 2 * c + 2) if c < 2 else (VS, VS)
            for m in range(lo, hi):
                heavy.append(("w", m + 1))
                heavy += [("v", m * KT // VS + k, z) for k in range(KT // VS) for z in range(2)]
    if not weigh:
        heavy.append(("w", VS))
    if not build:
        return heavy
    cost = {"a": 2, "v": 1}
    skip = 0 if gg else 1 + max([i for i, x in enumerate(heavy) if x[0] == "v"], default=2)
    total = sum(cost.get(x[0], 0) for x in heavy[skip:])
    n, w = sum(map(sum, UNITS[:gg])), sum(map(len, UNITS[:gg]))
    count = sum(UNITS[gg])
    starts = {n + sum(UNITS[gg][:k]): w + k for k in range(len(UNITS[gg]))}
    out, at, led, done = [], 0, 0, 0

    def lead(upto):
        nonlocal led
        while led < min(upto, count):
            if n + led in starts:
                out.append(("s", starts[n + led]))
            out.append(("h", n + led))
            led += 1

    for i, step in enumerate(heavy):
        now = 0
        if i >= skip:
            at += cost.get(step[0], 0)
            now = max(0, -(-count * at // total) - done)
            if now:
                lead(done + now + LEAD)
        elif step[0] in "av":
            lead(LEAD)
        out.append(step)
        out += [("b", done + n + k) for k in range(now)]
        done += now
    assert done == count and led == count
    return out


def build_steps():
    out = []
    for gg in range(GROUPS):
        out += [x for x in group_steps(gg, True, False) if x[0] in "shb"]
    return out


def rope_tables():
    half = HD // 2
    inv = np.power(np.float32(10000.0), -np.arange(half, dtype=np.float32) * np.float32(2.0 / HD))
    pos = np.zeros((TILES, P), np.float32)
    pos[:4] = np.arange(SEQ, dtype=np.float32).reshape(4, P)
    pos[4, :NS] = PAST + np.tile(np.arange(DEC_T, dtype=np.float32), DEC_B)
    ang = (pos[:, :, None] * inv.astype(np.float32)).astype(np.float32)
    cos, sin = np.cos(ang).astype(np.float32), np.sin(ang).astype(np.float32)
    cos = np.concatenate([cos, cos], -1).transpose(1, 0, 2)
    sin = np.concatenate([-sin, sin], -1).transpose(1, 0, 2)
    return np.ascontiguousarray(cos), np.ascontiguousarray(sin)


def reach_count(dist):
    n = np.zeros(dist.shape, np.float64)
    for win, dil in DILATIONS:
        n += (dist >= 0) & (dist % dil == 0) & (dist // dil <= win // dil)
    return n


def added_mask(count):
    return np.where(count > 0, np.log(np.maximum(count, 1)) / SCALE, NEG).astype(np.float32)


def prompt_mask():
    t = np.arange(SEQ)
    m = added_mask(reach_count(t[:, None] - t[None, :]))
    return np.ascontiguousarray(m.reshape(4, P, SEQ).transpose(1, 0, 2))


def sample_mask():
    i = np.arange(DEC_T)
    cached = added_mask(reach_count(PAST + i[:, None] - np.arange(PAST)[None, :]))
    m = np.full((NH, DEC_T, DEC_B, NSK), NEG, np.float32)
    m[:, :, :, :PAST] = cached[None, :, None, :]
    new = added_mask(reach_count(i[:, None] - i[None, :]))
    for b in range(DEC_B):
        m[:, :, b, PAST + b * DEC_T:PAST + (b + 1) * DEC_T] = new[None]
    return np.ascontiguousarray(m.reshape(SROWS, DEC_B, NSK))


def cols(i):
    return slice(i * P, i * P + ROWS[i])


def spread(ap, shape):
    return ap.to_broadcast(shape)


def project(nc, d, s):
    with ExitStack() as ctx:
        sb = lambda n, sh, dt=F32: ctx.enter_context(nc.sbuf_tensor(n, sh, dt))
        sem = lambda n: ctx.enter_context(nc.semaphore(n))
        w = sb("w_in_sb", [P, NCB, KT, CB])
        xT = sb("xT", [P, KT, T])
        xtok = sb("xtok", [P, 2, D])
        sq = sb("sq", [P, D])
        g1 = sb("g1", [P, KT])
        ss = sb("ss", [P, TILES])
        rstd = sb("rstd1", [P, TILES])
        cos = sb("cos", [P, TILES, HD])
        sin = sb("sin", [P, TILES, HD])
        qk = sb("qk", [P, 2 * AW])
        rot = sb("rot", [P, 2 * AW])
        qkr = sb("qkr", [P, 2 * AW])
        u1 = sb("u1", [P, CH])
        sg = sb("sg", [P, CH])
        g = sb("g", [P, CH])
        proj_ps = [ctx.enter_context(nc.psum_tensor(f"proj{b}", [P, 512], F32)) for b in range(4)]
        turn_ps = [ctx.enter_context(nc.psum_tensor(f"turn{b}", [P, 512], F32)) for b in range(4)]

        ident_in = sem("ident_in")
        x0_in, x_in, tab_in, hist_in = sem("x0_in"), sem("x_in"), sem("tab_in"), sem("hist_in")
        w_loaded = [sem(f"w_in{n}") for n in range(NCB)]
        squared, meaned, rooted, rstd_ready = sem("squared"), sem("meaned"), sem("rooted"), sem("rstd_ready")
        xg_ready = sem("xg_ready")
        xtok_in = [sem(f"xtok_in{b}") for b in range(2)]
        block_done, evacuated = sem("block_done"), sem("evacuated")
        rot_ready, cos_ready, roped = sem("rot_ready"), sem("cos_ready"), sem("roped")
        g_ready = sem("g_ready")
        turned, turn_read = sem("turned"), sem("turn_read")
        kept_stored, k_stored, v_stored, g_stored = (sem(x + "_stored") for x in ("kept", "k", "v", "g"))
        hist_zero = sem("hist_zero")
        ss_set = sem("ss_set")
        block = ctx.enter_context(nc.Block())
        NQK = 2 * AW // CB
        ident, qT, kT, v, gp, gs = s.ident, s.qT, s.kT, s.v, s.gp, s.gs

        @block.sync
        def _(sp):
            sp.dma_start(g1[:], d.g1).then_inc(tab_in, 16)
            sp.dma_start(xT[:, :, cols(0)], d.xT[:, :, cols(0)]).then_inc(x0_in, 16)
            for n in range(NCB):
                sp.dma_start(w[:, n], d.w_in[n]).then_inc(w_loaded[n], 16)
                if n == 1:
                    sp.dma_start(xT[:, :, P:T], d.xT[:, :, P:T]).then_inc(x_in, 16)
            sp.dma_start(gs[:, :, :, 0:TAPS - 1], d.state).then_inc(hist_in, 16)
            sp.dma_start(d.out_cs[:, 0:TAPS - 1 - DEC_T], d.state_rows[:, DEC_T:TAPS - 1]).then_inc(kept_stored, 16)
            for i in range(TILES):
                r = ROWS[i]
                sp.wait_ge(roped, i + 1)
                sp.dma_start(d.out_k[i * P:i * P + r], qkr[0:r, AW:]).then_inc(k_stored, 16)
                sp.wait_ge(evacuated, NCB * i + 9)
                sp.dma_start(d.out_v[i * P:i * P + r], v[0:r, i]).then_inc(v_stored, 16)
                if i >= 3:
                    sp.wait_ge(g_ready, i + 1)
                    if i == 3:
                        sp.dma_start(d.out_cp, g[P - (TAPS - 1):P]).then_inc(g_stored, 16)
                    else:
                        sp.dma_start(d.out_cs[:, TAPS - 1 - DEC_T:], g[0:NS]).then_inc(g_stored, 16)
            sp.wait_ge(kept_stored, 16)
            sp.wait_ge(k_stored, 16 * TILES)
            sp.wait_ge(v_stored, 16 * TILES)
            sp.wait_ge(g_stored, 32)
            sp.wait_ge(hist_in, 16)

        @block.scalar
        def _(act):
            act.dma_start(xtok[:, 0], d.x[0:P]).then_inc(xtok_in[0], 16)
            act.dma_start(xtok[:, 1], d.x[P:2 * P]).then_inc(xtok_in[1], 16)
            act.dma_start(cos[:], d.cos).then_inc(tab_in, 16)
            act.dma_start(sin[:], d.sin).then_inc(tab_in, 16)
            act.dma_start(ident[:], d.ident).then_inc(ident_in, 16)
            act.wait_ge(ss_set, 1)
            for i in range(TILES):
                r = ROWS[i]
                act.wait_ge(xtok_in[i % 2], 16 * (i // 2 + 1))
                if i:
                    act.wait_ge(squared, i)
                nc.scalar.activation(sq[0:r], xtok[0:r, i % 2], ACT.Square,
                                     accum_out=ss[0:r, i:i + 1]).then_inc(squared, 1)
                if i + 2 < TILES:
                    act.wait_ge(squared, i + 1)
                    act.dma_start(xtok[0:ROWS[i + 2], i % 2],
                                  d.x[(i + 2) * P:(i + 2) * P + ROWS[i + 2]]).then_inc(xtok_in[i % 2], 16)
            act.wait_ge(meaned, 1)
            nc.scalar.activation(rstd[:], ss[:], ACT.Sqrt).then_inc(rooted, 1)
            act.wait_ge(rstd_ready, 1)
            for i in range(TILES):
                r = ROWS[i]
                for n in range(NCB):
                    u = NCB * i + n
                    act.wait_ge(block_done, u + 1)
                    src = proj_ps[u % 4][0:r, 0:CB]
                    sc = rstd[0:r, i:i + 1]
                    if n < NQK:
                        if n == 0 and i:
                            act.wait_ge(cos_ready, i)
                        dst = qk[0:r, n * CB:(n + 1) * CB]
                    elif n < 9:
                        dst = v[0:r, i, (n - NQK) * CB:(n - NQK + 1) * CB]
                    else:
                        if n == 9 and i:
                            act.wait_ge(g_ready, i)
                        dst = (u1 if n == 9 else sg)[0:r]
                    f = ACT.Sigmoid if n == 10 else ACT.Copy
                    nc.scalar.activation(dst, src, f, scale=sc).then_inc(evacuated, 1)

        @block.vector
        def _(dve):
            nc.vector.memset(ss[:], 1.0).then_inc(ss_set, 1)
            nc.vector.memset(gp[:, :, 0:TAPS - 1], 0.0).then_inc(hist_zero, 1)
            dve.wait_ge(tab_in, 48)
            dve.wait_ge(x0_in, 16)

            def scale_x(a, b):
                nc.vector.tensor_tensor(xT[:, :, a:b], xT[:, :, a:b],
                                        spread(g1[:].rearrange("p (k o) -> p k o", o=1), [P, KT, b - a]),
                                        ALU.mult).then_inc(xg_ready, 1)

            scale_x(0, P)
            dve.wait_ge(squared, TILES)
            nc.vector.tensor_scalar(ss[:], ss[:], 1.0 / D, RMS_EPS, ALU.mult, ALU.add).then_inc(meaned, 1)
            dve.wait_ge(rooted, 1)
            nc.vector.reciprocal(rstd[:], rstd[:]).then_inc(rstd_ready, 1)
            dve.wait_ge(x_in, 16)
            scale_x(P, T)

            def rope(i):
                r = ROWS[i]
                x4 = qk[0:r].rearrange("p (h s e) -> p h s e", s=2, e=HD // 2)
                o4 = rot[0:r].rearrange("p (h s e) -> p h s e", s=2, e=HD // 2)
                n = 2 * NH
                dve.wait_ge(evacuated, NCB * i + NQK)
                if i:
                    dve.wait_ge(roped, i)
                for half in range(2):
                    sn = sin[0:r, i, half * 32:half * 32 + 32].rearrange("p (o e) -> p o e", o=1)
                    nc.vector.tensor_tensor(o4[:, :, half], x4[:, :, 1 - half], spread(sn, [r, n, HD // 2]),
                                            ALU.mult).then_inc(rot_ready, 1)
                if i:
                    dve.wait_ge(turned, 4 * i)
                    dve.wait_ge(k_stored, 16 * i)
                cs = cos[0:r, i].rearrange("p (o e) -> p o e", o=1)
                nc.vector.tensor_tensor(qkr[0:r].rearrange("p (h e) -> p h e", e=HD),
                                        qk[0:r].rearrange("p (h e) -> p h e", e=HD),
                                        spread(cs, [r, n, HD]), ALU.mult).then_inc(cos_ready, 1)
                dve.wait_ge(cos_ready, i + 1)
                dve.wait_ge(rot_ready, 2 * (i + 1))
                nc.vector.tensor_tensor(qkr[0:r], qkr[0:r], rot[0:r], ALU.add).then_inc(roped, 1)
                dve.wait_ge(evacuated, NCB * (i + 1))
                if i == 4:
                    dve.wait_ge(g_stored, 16)
                nc.vector.tensor_tensor(g[0:r], u1[0:r], sg[0:r], ALU.mult).then_inc(g_ready, 1)

            def take(i):
                r = ROWS[i]
                for b in range(4):
                    dve.wait_ge(turned, 4 * i + b + 1)
                    src = turn_ps[b][:, 0:4 * r].rearrange("p (j t) -> p j t", t=r)
                    if b < 3:
                        for j in range(4):
                            m = 4 * b + j
                            dst = (qT if m < PAIRS else kT)[:, m % PAIRS, cols(i)]
                            ins = nc.vector.tensor_copy(dst, src[:, j])
                    elif i < 4:
                        ins = nc.vector.tensor_copy(gp[:, :, TAPS - 1 + i * P:TAPS - 1 + (i + 1) * P], src[:, 0:2])
                    else:
                        ins = nc.vector.tensor_copy(gs[:, :, :, TAPS - 1:],
                                                    src[:, 0:2].rearrange("p c (b t) -> p c b t", t=DEC_T))
                    ins.then_inc(turn_read, 1)

            for i in range(TILES):
                rope(i)
                take(i)

        @block.tensor
        def _(pe):
            def turn(i):
                r = ROWS[i]
                if i == 0:
                    pe.wait_ge(ident_in, 16)
                for b in range(4):
                    if b == 0:
                        pe.wait_ge(roped, i + 1)
                    if b == 3:
                        pe.wait_ge(g_ready, i + 1)
                    if i:
                        pe.wait_ge(turn_read, 4 * (i - 1) + b + 1)
                    for j in range(4 if b < 3 else 2):
                        src = qkr[0:r, (4 * b + j) * P:(4 * b + j + 1) * P] if b < 3 else g[0:r, j * P:(j + 1) * P]
                        ins = pe.transpose(turn_ps[b][:, j * r:(j + 1) * r], src, ident[0:r, 0:r])
                    ins.then_inc(turned, 1)

            for i in range(TILES):
                pe.wait_ge(xg_ready, 1 if i == 0 else 2)
                for n in range(NCB):
                    u = NCB * i + n
                    if i == 0:
                        pe.wait_ge(w_loaded[n], 16)
                    if u >= 4:
                        pe.wait_ge(evacuated, u - 3)
                    for k in range(KT):
                        ins = pe.matmul(proj_ps[u % 4][0:ROWS[i], 0:CB], xT[:, k, cols(i)], w[:, n, k],
                                        start=(k == 0), stop=(k == KT - 1))
                    ins.then_inc(block_done, 1)
                    if n == 5 and i:
                        turn(i - 1)
            turn(TILES - 1)


def mix(nc, d, s):
    units = [(i, h) for i in range(4) for h in range(NH)] + [(4, b) for b in range(DEC_B)]
    U = len(units)
    UP = 4 * NH
    RING = 4

    def keys(u):
        return (units[u][0] + 1) * P if u < UP else NSK

    def rows(u):
        return P if u < UP else SROWS

    with ExitStack() as ctx:
        sb = lambda n, sh, dt=F32: ctx.enter_context(nc.sbuf_tensor(n, sh, dt))
        sem = lambda n: ctx.enter_context(nc.semaphore(n))
        pmask = sb("pmask", [P, 4, SEQ])
        smask = sb("smask", [SROWS, DEC_B, NSK])
        ckT = sb("ckT", [P, RING, PAIRS, PAST])
        cv = sb("cv", [P, RING, 2, AW])
        qbd = sb("qbd", [P, DEC_B, PAIRS, SROWS])
        sm = sb("sm", [P, 3, SEQ])
        pr = sb("pr", [P, 3, SEQ])
        prT = sb("prT", [P, 3, SEQ])
        mx = sb("mx", [P, U])
        nmx = sb("nmx", [P, U])
        den = sb("den", [P, U])
        rden = sb("rden", [P, U])
        attn = sb("attn", [P, 2, AW])
        cw = sb("cw", [P, 2, TAPS])
        cb = sb("cb", [P, 2])
        lng = sb("lng", [P, CH])
        lnb = sb("lnb", [P, CH])
        y = sb("y", [P, 2, T])
        yn = sb("yn", [P, TILES, CH])
        ysig = sb("ysig", [P, TILES, CH])
        st = sb("st", [P, TILES, 6])
        mv = sb("mv", [P, TILES, 2])
        lr = sb("lr", [P, TILES])
        s_ps = [ctx.enter_context(nc.psum_tensor(f"s_ps{b}", [P, 512], F32)) for b in range(3)]
        t_ps = [ctx.enter_context(nc.psum_tensor(f"t_ps{b}", [P, 512], F32)) for b in range(2)]
        o_ps = [ctx.enter_context(nc.psum_tensor(f"o_ps{b}", [P, 512], F32)) for b in range(2)]
        c_ps = ctx.enter_context(nc.psum_tensor("c_ps", [P, 512], F32))

        mask_in, conv_in, ln_in = sem("mask_in"), sem("conv_in"), sem("ln_in")
        cache_in = [sem(f"cache_in{b}") for b in range(RING)]
        qbd_zero, qbd_ready = sem("qbd_zero"), sem("qbd_ready")
        scored, maxed, neg_ready, exped = sem("scored"), sem("maxed"), sem("neg_ready"), sem("exped")
        rden_ready, scaled = sem("rden_ready"), sem("scaled")
        turned, copied, summed, normed = sem("turned"), sem("copied"), sem("summed"), sem("normed")
        cat_turned, cat_taken = sem("cat_turned"), sem("cat_taken")
        tapped = sem("tapped")
        y_turned, stats, aggr, eps_added = sem("y_turned"), sem("stats"), sem("aggr"), sem("eps_added")
        rooted, lr_ready, centred = sem("rooted"), sem("lr_ready"), sem("centred")
        gained, biased, sig_ready, gated = sem("gained"), sem("biased"), sem("sig_ready"), sem("gated")
        g_turned, g_taken = sem("g_turned"), sem("g_taken")
        block = ctx.enter_context(nc.Block())
        ident, qT, kT, v, gp, gs, catT = s.ident, s.qT, s.kT, s.v, s.gp, s.gs, s.catT

        @block.sync
        def _(sp):
            sp.dma_start(pmask[:], d.pmask).then_inc(mask_in, 16)
            sp.dma_start(smask[:], d.smask).then_inc(mask_in, 16)
            sp.dma_start(cw[:], d.conv_w).then_inc(conv_in, 16)
            sp.dma_start(cb[:], d.conv_b).then_inc(conv_in, 16)
            sp.dma_start(lng[:], spread(d.ln_g, [P, CH])).then_inc(ln_in, 16)
            sp.dma_start(lnb[:], spread(d.ln_b, [P, CH])).then_inc(ln_in, 16)
            for b in range(DEC_B):
                if b >= RING:
                    sp.wait_ge(summed, UP + b - RING + 1)
                sp.dma_start(ckT[:, b % RING], d.ckT[b]).then_inc(cache_in[b % RING], 16)
                sp.dma_start(cv[:, b % RING], d.cv[b]).then_inc(cache_in[b % RING], 16)

        @block.gpsimd
        def _(pool):
            nc.gpsimd.memset(qbd[:], 0.0).then_inc(qbd_zero, 1)
            pool.wait_ge(qbd_zero, 1)
            for j in range(PAIRS):
                for hh in range(2):
                    a, r0 = 64 * hh, 8 * j + 4 * hh
                    nc.gpsimd.tensor_copy(qbd[a:a + 64, :, j, r0:r0 + DEC_T],
                                          qT[a:a + 64, j, SEQ:T].rearrange("p (b t) -> p b t", t=DEC_T)
                                          ).then_inc(qbd_ready, 1)

        @block.tensor
        def _(pe):
            def score(u):
                i, h = units[u]
                if u >= 3:
                    pe.wait_ge(maxed, u - 2)
                n = keys(u)
                if u < UP:
                    a = 64 * (h % 2)
                    ins = pe.matmul(s_ps[u % 3][:, 0:n], qT[a:a + 64, h // 2, cols(i)], kT[a:a + 64, h // 2, 0:n],
                                    start=True, stop=True)
                else:
                    if u == UP:
                        pe.wait_ge(qbd_ready, 2 * PAIRS)
                    pe.wait_ge(cache_in[h % RING], 32 * (h // RING + 1))
                    for lo, hi in ((0, PAST), (PAST, NSK)):
                        for j in range(PAIRS):
                            rhs = ckT[:, h % RING, j] if lo == 0 else kT[:, j, SEQ:T]
                            ins = pe.matmul(s_ps[u % 3][0:SROWS, lo:hi], qbd[:, h, j], rhs,
                                            start=(j == 0), stop=(j == PAIRS - 1))
                ins.then_inc(scored, 1)

            def turn(u):
                if u < UP:
                    pe.wait_ge(exped, u + 1)
                else:
                    pe.wait_ge(scaled, u - UP + 1)
                if u >= 2:
                    pe.wait_ge(copied, u - 1)
                r, n = rows(u), keys(u)
                for q in range(0, n, P):
                    m = min(P, n - q)
                    c = q // P * r
                    ins = pe.transpose(t_ps[u % 2][0:m, c:c + r], pr[0:r, u % 3, q:q + m], ident[0:r, 0:r])
                ins.then_inc(turned, 1)

            def weigh(u):
                i, h = units[u]
                pe.wait_ge(copied, u + 1)
                if u >= 2:
                    pe.wait_ge(normed, u - 1)
                if u < UP:
                    for q in range(i + 1):
                        ins = pe.matmul(o_ps[u % 2][:, 0:HD], prT[:, u % 3, q * P:(q + 1) * P],
                                        v[:, q, h * HD:(h + 1) * HD], start=(q == 0), stop=(q == i))
                else:
                    for j in range(PAIRS):
                        for q in range(3):
                            m = P if q < 2 else NS
                            val = cv[:, h % RING, q, j * P:(j + 1) * P] if q < 2 else v[0:NS, 4, j * P:(j + 1) * P]
                            c = q * SROWS + 8 * j
                            ins = pe.matmul(o_ps[u % 2][:, 8 * j:8 * j + 8], val, prT[0:m, u % 3, c:c + 8],
                                            start=(q == 0), stop=(q == 2))
                ins.then_inc(summed, 1)

            def turn_cat(i, b):
                pe.wait_ge(normed, NH * (i + 1))
                if 2 * i + b:
                    pe.wait_ge(cat_taken, 2 * i + b)
                for j in range(4 * b, min(4 * b + 4, PAIRS)):
                    ins = pe.transpose(c_ps[:, (j - 4 * b) * P:(j - 4 * b + 1) * P], attn[:, i % 2, j * P:(j + 1) * P],
                                       ident[:])
                ins.then_inc(cat_turned, 1)

            for t in range(U + 3):
                if t < U:
                    score(t)
                if 0 <= t - 2 < U:
                    turn(t - 2)
                if 0 <= t - 3 < U:
                    weigh(t - 3)
                if t >= 16 and (t - 16) % NH < 2 and (t - 16) // NH < 4:
                    turn_cat((t - 16) // NH, (t - 16) % NH)
            pe.wait_ge(maxed, U)
            pe.wait_ge(tapped, 4 * TAPS)
            for i in range(TILES):
                for c in range(2):
                    at = (i % 2) * CH + c * P
                    ins = pe.transpose(s_ps[i // 2][0:ROWS[i], at:at + P], y[:, c, cols(i)], ident[:])
                ins.then_inc(y_turned, 1)
            for i in range(TILES):
                r = ROWS[i]
                pe.wait_ge(gated, i + 1)
                if i == 0:
                    pe.wait_ge(copied, U)
                if i >= 2:
                    pe.wait_ge(g_taken, i - 1)
                for c in range(2):
                    ins = pe.transpose(t_ps[i % 2][:, c * r:(c + 1) * r], yn[0:r, i, c * P:(c + 1) * P],
                                       ident[0:r, 0:r])
                ins.then_inc(g_turned, 1)

        @block.scalar
        def _(act):
            def exp(u):
                r, n = rows(u), keys(u)
                act.wait_ge(neg_ready, u + 1)
                if u >= 3:
                    act.wait_ge(turned, u - 2)
                nc.scalar.activation(pr[0:r, u % 3, 0:n], sm[0:r, u % 3, 0:n], ACT.Exp, bias=nmx[0:r, u:u + 1],
                                     scale=SCALE, accum_out=den[0:r, u:u + 1]).then_inc(exped, 1)

            def copy(u):
                act.wait_ge(turned, u + 1)
                if u >= 3:
                    act.wait_ge(summed, u - 2)
                if u < UP:
                    n = keys(u)
                    nc.scalar.copy(prT[:, u % 3, 0:n], t_ps[u % 2][:, 0:n]).then_inc(copied, 1)
                else:
                    nc.scalar.copy(prT[:, u % 3, 0:2 * SROWS], t_ps[u % 2][:, 0:2 * SROWS])
                    nc.scalar.copy(prT[0:NS, u % 3, 2 * SROWS:3 * SROWS],
                                   t_ps[u % 2][0:NS, 2 * SROWS:3 * SROWS]).then_inc(copied, 1)

            for t in range(U + 2):
                if t < U:
                    exp(t)
                if t >= 2:
                    copy(t - 2)
            act.wait_ge(eps_added, 1)
            nc.scalar.activation(lr[:], lr[:], ACT.Sqrt).then_inc(rooted, 1)
            for i in range(TILES):
                act.wait_ge(biased, i + 1)
                nc.scalar.activation(ysig[0:ROWS[i], i], yn[0:ROWS[i], i], ACT.Sigmoid).then_inc(sig_ready, 1)

        @block.vector
        def _(dve):
            def row_max(u):
                i, h = units[u]
                r, n = rows(u), keys(u)
                dve.wait_ge(scored, u + 1)
                if u == 0:
                    dve.wait_ge(mask_in, 32)
                if u >= 3:
                    dve.wait_ge(exped, u - 2)
                mask = pmask[:, i, 0:n] if u < UP else smask[:, h]
                nc.vector.tensor_tensor_reduce(out=sm[0:r, u % 3, 0:n], in0=s_ps[u % 3][0:r, 0:n], in1=mask,
                                               scale=1.0, scalar=-3.0e38, op0=ALU.add, op1=ALU.max,
                                               accum_out=mx[0:r, u:u + 1]).then_inc(maxed, 1)
                dve.wait_ge(maxed, u + 1)
                nc.vector.tensor_scalar(nmx[0:r, u:u + 1], mx[0:r, u:u + 1], -SCALE, None,
                                        ALU.mult).then_inc(neg_ready, 1)

            def inverse(u):
                r, n = rows(u), keys(u)
                dve.wait_ge(exped, u + 1)
                nc.vector.reciprocal(rden[0:r, u:u + 1], den[0:r, u:u + 1]).then_inc(rden_ready, 1)
                if u >= UP:
                    dve.wait_ge(rden_ready, u + 1)
                    nc.vector.tensor_scalar(pr[0:r, u % 3, 0:n], pr[0:r, u % 3, 0:n], rden[0:r, u:u + 1], None,
                                            ALU.mult).then_inc(scaled, 1)

            def norm(u):
                i, h = units[u]
                dve.wait_ge(summed, u + 1)
                if u < UP:
                    dve.wait_ge(rden_ready, u + 1)
                    if h == 0 and i >= 2:
                        dve.wait_ge(cat_turned, 2 * (i - 1))
                    nc.vector.tensor_scalar(attn[:, i % 2, h * HD:(h + 1) * HD], o_ps[u % 2][:, 0:HD],
                                            rden[:, u:u + 1], None, ALU.mult).then_inc(normed, 1)
                else:
                    for hh in range(2):
                        a = 64 * hh
                        src = o_ps[u % 2][a:a + 64, 0:SROWS].rearrange("p (j c) -> p j c", c=8)
                        ins = nc.vector.tensor_copy(catT[a:a + 64, 0:PAIRS, SEQ + DEC_T * h:SEQ + DEC_T * (h + 1)],
                                                    src[:, :, 4 * hh:4 * hh + 4])
                    ins.then_inc(normed, 1)

            def take_cat(i, b):
                dve.wait_ge(cat_turned, 2 * i + b + 1)
                n = 4 if b == 0 else 2
                nc.vector.tensor_copy(catT[:, 4 * b:4 * b + n, cols(i)],
                                      c_ps[:, 0:n * P].rearrange("p (j t) -> p j t", t=P)).then_inc(cat_taken, 1)

            def tap(k):
                for c in range(2):
                    for part in range(2):
                        if part == 0:
                            src, acc = gp[:, c, k:k + SEQ], y[:, c, 0:SEQ]
                        else:
                            src = gs[:, c, :, k:k + DEC_T]
                            acc = y[:, c, SEQ:T].rearrange("p (b t) -> p b t", t=DEC_T)
                        w = cw[:, c, k:k + 1]
                        if k == 0:
                            nc.vector.tensor_scalar(acc, src, w, cb[:, c:c + 1], ALU.mult, ALU.add
                                                    ).then_inc(tapped, 1)
                        else:
                            dve.wait_ge(tapped, 4 * k - 3 + 2 * c + part)
                            nc.vector.scalar_tensor_tensor(out=acc, in0=src, scalar=w, in1=acc, op0=ALU.mult,
                                                           op1=ALU.add).then_inc(tapped, 1)

            dve.wait_ge(conv_in, 32)
            for t in range(U + 4):
                if t < U:
                    row_max(t)
                if 0 <= t - 1 < U:
                    inverse(t - 1)
                if t < TAPS:
                    tap(t)
                if 0 <= t - 4 < U:
                    norm(t - 4)
                if t >= 16 and (t - 16) % NH < 2 and (t - 16) // NH < 4:
                    take_cat((t - 16) // NH, (t - 16) % NH)
            nc.vector.memset(lr[:], 1.0).then_inc(stats, 1)
            for i in range(TILES):
                r = ROWS[i]
                dve.wait_ge(y_turned, min(i // 2 * 2 + 2, TILES))
                nc.vector.bn_stats(st[0:r, i], s_ps[i // 2][0:r, (i % 2) * CH:(i % 2 + 1) * CH]).then_inc(stats, 1)
            for i in range(TILES):
                dve.wait_ge(stats, i + 2)
                nc.vector.bn_aggr(mv[0:ROWS[i], i], st[0:ROWS[i], i]).then_inc(aggr, 1)
            dve.wait_ge(aggr, TILES)
            nc.vector.tensor_scalar(lr[:, 0:4], mv[:, 0:4, 1], LN_EPS, None, ALU.add)
            nc.vector.tensor_scalar(lr[0:NS, 4:5], mv[0:NS, 4, 1:2], LN_EPS, None, ALU.add).then_inc(eps_added, 1)
            dve.wait_ge(rooted, 1)
            nc.vector.reciprocal(lr[:], lr[:]).then_inc(lr_ready, 1)
            dve.wait_ge(lr_ready, 1)
            for i in range(TILES):
                r = ROWS[i]
                nc.vector.tensor_scalar(yn[0:r, i], s_ps[i // 2][0:r, (i % 2) * CH:(i % 2 + 1) * CH],
                                        mv[0:r, i, 0:1], lr[0:r, i:i + 1], ALU.subtract, ALU.mult
                                        ).then_inc(centred, 1)
            dve.wait_ge(ln_in, 32)
            for i in range(TILES):
                r = ROWS[i]
                dve.wait_ge(centred, i + 1)
                nc.vector.tensor_tensor(yn[0:r, i], yn[0:r, i], lng[0:r], ALU.mult).then_inc(gained, 1)
            for i in range(TILES):
                r = ROWS[i]
                dve.wait_ge(gained, i + 1)
                nc.vector.tensor_tensor(yn[0:r, i], yn[0:r, i], lnb[0:r], ALU.add).then_inc(biased, 1)
            for i in range(TILES):
                r = ROWS[i]
                dve.wait_ge(sig_ready, i + 1)
                nc.vector.tensor_tensor(yn[0:r, i], yn[0:r, i], ysig[0:r, i], ALU.mult).then_inc(gated, 1)
            for i in range(TILES):
                r = ROWS[i]
                dve.wait_ge(g_turned, i + 1)
                nc.vector.tensor_copy(catT[:, PAIRS:KT, cols(i)],
                                      t_ps[i % 2][:, 0:2 * r].rearrange("p (c t) -> p c t", t=r)).then_inc(g_taken, 1)


def over(nc, stack, name, name_r, shape):
    at = -(-nc.sbuf_base // 32) * 32
    return (stack.enter_context(nc.sbuf_tensor(name, shape, F32)),
            nc.alloc_sbuf_tensor_at(name_r, shape, F32R, offset=at))


def wait(eng, sem, value):
    if not (isinstance(value, int) and value <= 0):
        eng.wait_ge(sem, value)


def choose(nc, d, s):
    with ExitStack() as ctx:
        sb = lambda n, sh, dt=F32: ctx.enter_context(nc.sbuf_tensor(n, sh, dt))
        sem = lambda n: ctx.enter_context(nc.semaphore(n))
        wo = sb("wo", [P, KT, D])
        x1 = sb("x1", [P, TILES, D])
        xr = sb("xr", [P, 2, D])
        g2 = sb("g2", [P, KT])
        ss = sb("ss2", [P, TILES])
        rt = sb("rt2", [P, TILES])
        wq = sb("wq", [P, 4, KT, P])
        keysT = sb("keysT", [P, 2, NK])
        qh = sb("qh", [P, 4, T])
        sc = sb("sc", [P, 2, TILES, 2, NK])
        v16 = sb("v16", [P, 2, TILES, 2, TOPK])
        i16 = sb("i16", [P, 2, TILES, 2, TOPK], U32)
        cand = sb("cand", [P, 2, TILES, TOPK * TOPK])
        top = sb("top", [P, 2, TILES, TOPK])
        ci = sb("ci", [P, 2, TILES, TOPK], U32)
        cab = sb("cab", [P, 2, 2, TILES, TOPK], U32)
        hit = sb("hit", [P, 2, TILES, TOPK, TOPK])
        iota = sb("iota", [P, TOPK])
        keyf = sb("keyf", [P, 2, 2, TILES, TOPK])
        tops = sb("tops", [P, TILES, PH, TOPK])
        ef = sb("ef", [P, 2, TILES, PH, TOPK])
        gsum = sb("gsum", [P, TILES, PH])
        shift = sb("shift", [P, TILES, PH, TOPK])
        wf = sb("wf", [P, T])
        rest = sb("rest", [P, T])
        banks = [ctx.enter_context(nc.psum_tensor(f"bank{b}", [P, 512], F32)) for b in range(8)]

        wo_in, x_in, g2_in, keys_in, iota_in = sem("wo_in"), sem("x1_in"), sem("g2_in"), sem("keys_in"), sem("iota_in")
        wq_in = [sem(f"wq_in{b}") for b in range(4)]
        outed, added, squared, meaned = sem("outed"), sem("added"), sem("squared"), sem("meaned")
        rooted, inverted, scaled = sem("rooted"), sem("inverted"), sem("scaled")
        x_turned, h_taken = sem("x_turned"), sem("h_taken")
        x1_stored = sem("x1_stored")
        q_done, q_taken, s_done, s_taken = sem("q_done"), sem("q_taken"), sem("s_done"), sem("s_taken")
        half_step, cand_ready, top_step = sem("half_step"), sem("cand_ready"), sem("top_step")
        split_ready, hit_ready, picked, decoded = sem("split_ready"), sem("hit_ready"), sem("picked"), sem("decoded")
        shifted, gate_exp, gate_sum, gate_inv, gates = (sem(x) for x in ("shifted", "gate_exp", "gate_sum",
                                                                          "gate_inv", "gates"))
        first_half_done, tops_kept, sub_ready = sem("first_half_done"), sem("tops_kept"), sem("sub_ready")
        slot_turned, slot_taken, w_step = sem("slot_turned"), sem("slot_taken"), sem("w_step")
        block = ctx.enter_context(nc.Block())
        ident, catT, h2T, e1T, e2T, w3 = s.ident, s.catT, s.h2T, s.e1T, s.e2T, s.w3
        HALVES = 10
        TOPS = 5

        @block.sync
        def _(sp):
            sp.dma_start(wo[:], d.w_out).then_inc(wo_in, 16)
            sp.dma_start(x1[:, 0:4], d.x[0:SEQ].rearrange("(i p) n -> p i n", p=P)).then_inc(x_in, 16)
            sp.dma_start(x1[0:NS, 4], d.x[SEQ:T]).then_inc(x_in, 16)
            sp.dma_start(g2[:], d.g2).then_inc(g2_in, 16)
            sp.dma_start(keysT[:], d.keysT).then_inc(keys_in, 16)
            sp.dma_start(iota[:], d.iota[:, 0:TOPK]).then_inc(iota_in, 16)

            def load(it):
                for b in range(4):
                    wait(sp, q_done, 4 * it + b - 3)
                    src = d.w_q[bass.ds(4 * it + b, 1)].rearrange("o p k n -> (o p) k n")
                    sp.dma_start(wq[:, b], src).then_inc(wq_in[b], 16)

            load(0)
            with sp.Fori(1, PH // 2) as it:
                load(it)
            sp.wait_ge(added, 2 * TILES)
            sp.dma_start(d.x1[0:SEQ].rearrange("(i p) n -> p i n", p=P), x1[:, 0:4]).then_inc(x1_stored, 16)
            sp.dma_start(d.x1[SEQ:T], x1[0:NS, 4]).then_inc(x1_stored, 16)
            sp.wait_ge(x1_stored, 32)

        @block.tensor
        def _(pe):
            def out_projection(i):
                for n in range(2):
                    b = 2 * (i % 2) + n
                    wait(pe, added, 2 * i + n - 3)
                    for k in range(KT):
                        ins = pe.matmul(banks[b][0:ROWS[i]], catT[:, k, cols(i)], wo[:, k, n * 512:(n + 1) * 512],
                                        start=(k == 0), stop=(k == KT - 1))
                    ins.then_inc(outed, 1)

            def turn(i):
                r = ROWS[i]
                pe.wait_ge(scaled, i + 1)
                for n in range(2):
                    b = 4 + 2 * (i % 2) + n
                    wait(pe, h_taken, 2 * i + n - 3)
                    for j in range(4):
                        k = 4 * n + j
                        ins = pe.transpose(banks[b][:, j * r:(j + 1) * r], xr[0:r, i % 2, k * P:(k + 1) * P],
                                           ident[0:r, 0:r])
                    ins.then_inc(x_turned, 1)

            pe.wait_ge(wo_in, 16)
            for i in range(TILES + 1):
                if i < TILES:
                    out_projection(i)
                if i:
                    turn(i - 1)
            pe.wait_ge(h_taken, 2 * TILES)
            pe.wait_ge(keys_in, 16)

            def head(it, hh):
                for half in range(2):
                    b = 2 * hh + half
                    pe.wait_ge(wq_in[b], 16 * (it + 1))
                    for z in range(2):
                        q = 4 * it + b
                        wait(pe, q_taken, 2 * q + z - 3)
                        for k in range(KT):
                            ins = pe.matmul(banks[2 * half + z][:, 0:HT], wq[:, b, k], h2T[:, k, z * HT:(z + 1) * HT],
                                            start=(k == 0), stop=(k == KT - 1))
                        if z == 1:
                            ins.then_inc(q_done, 1)
                        else:
                            ins.then_inc(first_half_done, 1)
                pe.wait_ge(q_taken, 4 * (2 * it + hh + 1))
                for i in range(TILES):
                    u = 5 * (2 * it + hh) + i
                    wait(pe, s_taken, u - 3)
                    for half in range(2):
                        ins = pe.matmul(banks[4 + (5 * hh + i) % 4][0:ROWS[i], half * NK:(half + 1) * NK],
                                        qh[:, 2 * hh + half, cols(i)], keysT[:, half], start=True, stop=True)
                    ins.then_inc(s_done, 1)

            for hh in range(2):
                head(0, hh)
            with pe.Fori(1, PH // 2) as it:
                for hh in range(2):
                    head(it, hh)
            pe.wait_ge(gates, 2)
            pe.wait_ge(decoded, 4 * PH)
            pe.wait_ge(s_taken, TILES * PH)
            for n in range(3):
                for i in range(TILES):
                    r = ROWS[i]
                    src = ef[0:r, n, i] if n < 2 else tops[0:r, i]
                    dst = banks[n][:, i * P:(i + 1) * P] if i < 4 else banks[3][:, n * NS:(n + 1) * NS]
                    ins = pe.transpose(dst, src.rearrange("p h k -> p (h k)"), ident[0:r, 0:r])
            ins.then_inc(slot_turned, 1)

        @block.scalar
        def _(act):
            for i in range(TILES):
                r = ROWS[i]
                act.wait_ge(added, 2 * (i + 1))
                if i >= 2:
                    act.wait_ge(x_turned, 2 * (i - 1))
                nc.scalar.activation(xr[0:r, i % 2], x1[0:r, i], ACT.Square, accum_out=ss[0:r, i:i + 1]
                                     ).then_inc(squared, 1)
                act.wait_ge(meaned, i + 1)
                nc.scalar.activation(rt[0:r, i:i + 1], ss[0:r, i:i + 1], ACT.Sqrt).then_inc(rooted, 1)
                act.wait_ge(inverted, i + 1)
                nc.scalar.activation(xr[0:r, i % 2], x1[0:r, i], ACT.Copy, scale=rt[0:r, i:i + 1]).then_inc(scaled, 1)

            def head(it, hh):
                for half in range(2):
                    b = 2 * hh + half
                    for z in range(2):
                        q = 4 * it + b
                        act.wait_ge(q_done if z else first_half_done, q + 1)
                        if not (isinstance(it, int) and it == 0):
                            act.wait_ge(s_done, TILES * (2 * it + hh - 1))
                        nc.scalar.copy(qh[:, b, z * HT:(z + 1) * HT], banks[2 * half + z][:, 0:HT]).then_inc(q_taken, 1)
                for i in range(TILES):
                    r = ROWS[i]
                    act.wait_ge(s_done, TILES * (2 * it + hh) + i + 1)
                    if not (isinstance(it, int) and it == 0):
                        act.wait_ge(half_step, HALVES * (TILES * (2 * it + hh - 2) + i + 1))
                    nc.scalar.copy(sc[0:r, hh, i].rearrange("p a n -> p (a n)"),
                                   banks[4 + (5 * hh + i) % 4][0:r, 0:2 * NK]).then_inc(s_taken, 1)

            for hh in range(2):
                head(0, hh)
            with act.Fori(1, PH // 2) as it:
                for hh in range(2):
                    head(it, hh)
            act.wait_ge(shifted, 2)
            nc.scalar.activation(tops[:, 0:4], tops[:, 0:4], ACT.Exp)
            nc.scalar.activation(tops[0:NS, 4], tops[0:NS, 4], ACT.Exp).then_inc(gate_exp, 1)

        @block.gpsimd
        def _(pool):
            def sums(it, hh, i):
                r = ROWS[i]
                u = TILES * (2 * it + hh) + i
                pool.wait_ge(half_step, HALVES * (u + 1))
                if not (isinstance(it, int) and it == 0):
                    pool.wait_ge(top_step, TOPS * (u - 2 * TILES + 1))
                a = v16[0:r, hh, i, 0].rearrange("p (a o) -> p a o", o=1)
                b = v16[0:r, hh, i, 1].rearrange("p (o b) -> p o b", o=1)
                nc.gpsimd.tensor_tensor(cand[0:r, hh, i].rearrange("p (a b) -> p a b", b=TOPK),
                                        spread(a, [r, TOPK, TOPK]), spread(b, [r, TOPK, TOPK]),
                                        ALU.add).then_inc(cand_ready, 1)

            def pick(it, hh):
                n = 2 * it + hh
                for half in range(2):
                    for part, (lo, hi, r) in enumerate(((0, 4, P), (4, 5, NS))):
                        pool.wait_ge(hit_ready, 4 * n + 2 * half + part + 1)
                        for i in range(lo, hi):
                            key = keyf[0:r, hh, half, i].rearrange("p (o k) -> p o k", o=1)
                            ins = nc.gpsimd.tensor_tensor(hit[0:r, half, i], hit[0:r, half, i],
                                                          spread(key, [r, TOPK, TOPK]), ALU.mult)
                        ins.then_inc(picked, 1)

            def head(it, hh):
                for i in range(TILES):
                    sums(it, hh, i)
                if hh == 0:
                    if not (isinstance(it, int) and it == 0):
                        pick(it - 1, 1)
                else:
                    pick(it, 0)

            for hh in range(2):
                head(0, hh)
            with pool.Fori(1, PH // 2) as it:
                for hh in range(2):
                    head(it, hh)
            pick(PH // 2 - 1, 1)

        @block.vector
        def _(dve):
            dve.wait_ge(x_in, 32)
            dve.wait_ge(g2_in, 16)
            dve.wait_ge(iota_in, 16)

            def take(i):
                r = ROWS[i]
                for n in range(2):
                    dve.wait_ge(x_turned, 2 * i + n + 1)
                    g = g2[:, 4 * n:4 * n + 4].rearrange("p (k o) -> p k o", o=1)
                    nc.vector.tensor_tensor(h2T[:, 4 * n:4 * n + 4, cols(i)],
                                            banks[4 + 2 * (i % 2) + n][:, 0:4 * r].rearrange("p (k t) -> p k t", t=r),
                                            spread(g, [P, 4, r]), ALU.mult).then_inc(h_taken, 1)

            for i in range(TILES):
                r = ROWS[i]
                for n in range(2):
                    dve.wait_ge(outed, 2 * i + n + 1)
                    nc.vector.tensor_tensor(x1[0:r, i, n * 512:(n + 1) * 512], x1[0:r, i, n * 512:(n + 1) * 512],
                                            banks[2 * (i % 2) + n][0:r], ALU.add).then_inc(added, 1)
                dve.wait_ge(squared, i + 1)
                nc.vector.tensor_scalar(ss[0:r, i:i + 1], ss[0:r, i:i + 1], 1.0 / D, RMS_EPS, ALU.mult, ALU.add
                                        ).then_inc(meaned, 1)
                dve.wait_ge(rooted, i + 1)
                nc.vector.reciprocal(rt[0:r, i:i + 1], rt[0:r, i:i + 1]).then_inc(inverted, 1)
                if i:
                    take(i - 1)
            take(TILES - 1)

            def search(it, hh, i):
                r = ROWS[i]
                u = TILES * (2 * it + hh) + i
                dve.wait_ge(s_taken, u + 1)
                if not (isinstance(it, int) and it == 0):
                    dve.wait_ge(cand_ready, u - 2 * TILES + 1)
                x = [sc[0:r, hh, i, half] for half in range(2)]
                val = [v16[0:r, hh, i, half] for half in range(2)]
                key = [i16[0:r, hh, i, half] for half in range(2)]
                base = HALVES * u
                for half in range(2):
                    nc.vector.max(val[half][:, 0:8], x[half]).then_inc(half_step, 1)
                for half in range(2):
                    dve.wait_ge(half_step, base + 1 + half)
                    nc.vector.max_index(key[half][:, 0:8], val[half][:, 0:8], x[half]).then_inc(half_step, 1)
                for half in range(2):
                    dve.wait_ge(half_step, base + 3 + half)
                    nc.vector.match_replace(x[half], val[half][:, 0:8], x[half], -3.0e38).then_inc(half_step, 1)
                for half in range(2):
                    dve.wait_ge(half_step, base + 5 + half)
                    nc.vector.max(val[half][:, 8:16], x[half]).then_inc(half_step, 1)
                for half in range(2):
                    dve.wait_ge(half_step, base + 7 + half)
                    nc.vector.max_index(key[half][:, 8:16], val[half][:, 8:16], x[half]).then_inc(half_step, 1)

            def search_sums(it, hh, i):
                r = ROWS[i]
                u = TILES * (2 * it + hh) + i
                dve.wait_ge(cand_ready, u + 1)
                x, val, at = cand[0:r, hh, i], top[0:r, hh, i], ci[0:r, hh, i]
                base = TOPS * u
                nc.vector.max(val[:, 0:8], x).then_inc(top_step, 1)
                dve.wait_ge(top_step, base + 1)
                nc.vector.max_index(at[:, 0:8], val[:, 0:8], x).then_inc(top_step, 1)
                dve.wait_ge(top_step, base + 2)
                nc.vector.match_replace(x, val[:, 0:8], x, -3.0e38).then_inc(top_step, 1)
                dve.wait_ge(top_step, base + 3)
                nc.vector.max(val[:, 8:16], x).then_inc(top_step, 1)
                dve.wait_ge(top_step, base + 4)
                nc.vector.max_index(at[:, 8:16], val[:, 8:16], x).then_inc(top_step, 1)

            def split(it, hh):
                n = 2 * it + hh
                dve.wait_ge(top_step, TOPS * TILES * (n + 1))
                dve.wait_ge(half_step, HALVES * TILES * (n + 1))
                if not (isinstance(it, int) and it == 0):
                    dve.wait_ge(picked, 4 * (n - 1))
                for half in range(2):
                    amount, op = (4, ALU.logical_shift_right) if half == 0 else (15, ALU.bitwise_and)
                    nc.vector.tensor_copy(keyf[:, hh, half, 0:4], i16[:, hh, 0:4, half])
                    nc.vector.tensor_copy(keyf[0:NS, hh, half, 4], i16[0:NS, hh, 4, half])
                    nc.vector.tensor_scalar(cab[:, hh, half, 0:4], ci[:, hh, 0:4], amount, None, op)
                    nc.vector.tensor_scalar(cab[0:NS, hh, half, 4], ci[0:NS, hh, 4], amount, None, op
                                            ).then_inc(split_ready, 1)
                for lo, hi, r in ((0, 4, P), (4, 5, NS)):
                    dst = tops[0:r, lo:hi, bass.ds(n, 1)].rearrange("p i o k -> p i (o k)")
                    nc.vector.tensor_copy(dst, top[0:r, hh, lo:hi]).then_inc(tops_kept, 1)

            def hits(it, hh):
                n = 2 * it + hh
                for half in range(2):
                    dve.wait_ge(split_ready, 2 * (n + 1))
                    wait(dve, decoded, 2 * (2 * n + half - 1))
                    for lo, hi, r in ((0, 4, P), (4, 5, NS)):
                        for i in range(lo, hi):
                            slot = cab[0:r, hh, half, i].rearrange("p (j o) -> p j o", o=1)
                            place = iota[0:r].rearrange("p (o k) -> p o k", o=1)
                            ins = nc.vector.tensor_tensor(hit[0:r, half, i], spread(slot, [r, TOPK, TOPK]),
                                                          spread(place, [r, TOPK, TOPK]), ALU.is_equal)
                        ins.then_inc(hit_ready, 1)

            def decode(it, hh):
                n = 2 * it + hh
                for half in range(2):
                    for g, (lo, hi, r) in enumerate(((0, 4, P), (4, 5, NS))):
                        dve.wait_ge(picked, 4 * n + 2 * half + g + 1)
                        dst = ef[0:r, half, lo:hi, bass.ds(n, 1)].rearrange("p i o k -> p i (o k)")
                        nc.vector.tensor_reduce(dst, hit[0:r, half, lo:hi], AX_X, ALU.add).then_inc(decoded, 1)

            def head(it, hh):
                first = isinstance(it, int) and it == 0
                for i in range(TILES):
                    search(it, hh, i)
                    if i:
                        search_sums(it, hh, i - 1)
                search_sums(it, hh, TILES - 1)
                split(it, hh)
                if hh == 1:
                    decode(it, 0)
                elif not first:
                    decode(it - 1, 1)
                hits(it, hh)

            for hh in range(2):
                head(0, hh)
            for it in range(1, PH // 2):
                for hh in range(2):
                    head(it, hh)
            decode(PH // 2 - 1, 1)
            dve.wait_ge(tops_kept, 2 * PH)
            parts = ((0, 4, P), (4, 5, NS))
            for lo, hi, r in parts:
                for i in range(lo, hi):
                    ins = nc.vector.tensor_tensor(shift[0:r, i], tops[0:r, i], spread(tops[0:r, i, :, 0:1], [r, PH, TOPK]),
                                                  ALU.subtract)
                ins.then_inc(sub_ready, 1)
            for n, (lo, hi, r) in enumerate(parts):
                dve.wait_ge(sub_ready, n + 1)
                nc.vector.tensor_copy(tops[0:r, lo:hi], shift[0:r, lo:hi]).then_inc(shifted, 1)
            dve.wait_ge(gate_exp, 1)
            for lo, hi, r in parts:
                nc.vector.tensor_reduce(gsum[0:r, lo:hi], tops[0:r, lo:hi], AX_X, ALU.add).then_inc(gate_sum, 1)
            for n, (lo, hi, r) in enumerate(parts):
                dve.wait_ge(gate_sum, n + 1)
                nc.vector.reciprocal(gsum[0:r, lo:hi], gsum[0:r, lo:hi]).then_inc(gate_inv, 1)
            for n, (lo, hi, r) in enumerate(parts):
                dve.wait_ge(gate_inv, n + 1)
                for i in range(lo, hi):
                    inv = gsum[0:r, i].rearrange("p (h o) -> p h o", o=1)
                    ins = nc.vector.tensor_tensor(tops[0:r, i], tops[0:r, i], spread(inv, [r, PH, TOPK]), ALU.mult)
                ins.then_inc(gates, 1)
            dve.wait_ge(slot_turned, 1)
            for n, dst in enumerate((e1T, e2T, wf)):
                nc.vector.tensor_copy(dst[:, 0:SEQ], banks[n][:])
                nc.vector.tensor_copy(dst[:, SEQ:T], banks[3][:, n * NS:(n + 1) * NS]).then_inc(slot_taken, 1)
            dve.wait_ge(slot_taken, 3)
            nc.vector.tensor_copy(w3[:, 0], wf[:]).then_inc(w_step, 1)
            dve.wait_ge(w_step, 1)
            nc.vector.tensor_tensor(rest[:], wf[:], w3[:, 0], ALU.subtract).then_inc(w_step, 1)
            dve.wait_ge(w_step, 2)
            nc.vector.tensor_copy(w3[:, 1], rest[:]).then_inc(w_step, 1)
            dve.wait_ge(w_step, 3)
            nc.vector.tensor_tensor(w3[:, 2], rest[:], w3[:, 1], ALU.subtract).then_inc(w_step, 1)


def experts(nc, d, s):
    with ExitStack() as ctx:
        sb = lambda n, sh, dt=F32: ctx.enter_context(nc.sbuf_tensor(n, sh, dt))
        sem = lambda n: ctx.enter_context(nc.semaphore(n))
        gate, p_high = over(nc, ctx, "gate", "p_high", [P, 2, CPP, T])
        p_low = sb("p_low", [P, 2 * CG, T], F32R)
        u, u_low = over(nc, ctx, "u", "u_low", [P, 2, KT, P])
        u_high = sb("u_high", [P, 2, KT, P], F32R)
        vv, v_low = over(nc, ctx, "vv", "v_low", [P, 2, CG, VC])
        v_high = sb("v_high", [P, 2, CG, VC], F32R)
        h_high = sb("h_high", [P, KT, T], F32R)
        gel = sb("gel", [P, 4, HT])
        hot = sb("hot", [P, HOTS, NK, TB], BF16)
        eq2 = sb("eq2", [P, CPP, UT_MAX], BF16)
        wsec = sb("wsec", [P, 2, 3, CPP, UT_MAX], BF16)
        iota_f = sb("iota_f", [P, NK])
        count_k = sb("count_k", [P, NK, TB], BF16)
        count_c = sb("count_c", [P, CPP, UT_MAX], BF16)
        a_ps = [ctx.enter_context(nc.psum_tensor(f"a_ps{b}", [P, 512], F32)) for b in range(2)]
        y_ps = [ctx.enter_context(nc.psum_tensor(f"y_ps{b}", [P, 512], F32)) for b in range(4)]
        g_ps = [ctx.enter_context(nc.psum_tensor(f"g_ps{b}", [P, 512], F32)) for b in range(2)]

        u_in = [sem(f"u_in{b}") for b in range(2)]
        v_in = [sem(f"v_in{b}") for b in range(2)]
        iota_in, consts = sem("iota_in"), sem("consts")
        a_done, acted, gated = sem("a_done"), sem("acted"), sem("gated")
        v_done, y_added = sem("v_done"), sem("y_added")
        eq_ready, w_ready = sem("eq_ready"), sem("w_ready")
        hot_ready, moved = sem("hot_ready"), sem("moved")
        g_done, built = sem("g_done"), sem("built")
        h_rounded, h_split = sem("h_rounded"), sem("h_split")
        u_rounded, u_split = sem("u_rounded"), sem("u_split")
        v_rounded, v_split = sem("v_rounded"), sem("v_split")
        p_rounded, p_split = sem("p_rounded"), sem("p_split")
        block = ctx.enter_context(nc.Block())
        h2T, h_low, e1T, e2T, w3, yT = s.h2T, s.h_low, s.e1T, s.e2T, s.w3, s.yT
        unit_of = [w for w, m in enumerate(m for g in UNITS for m in g) for _ in range(m)]
        unit_at = [unit_of.index(w) for w in range(UPP)]

        def slab(tensor, par, c, z):
            return tensor[:, bass.ds(par, 1), c, z * HT:(z + 1) * HT].rearrange("p o t -> p (o t)")

        def run_parts(eng, group):
            for gg in range(GROUPS):
                group(0, gg, True)
            with eng.Fori(1, PARTS - 1) as part:
                for gg in range(GROUPS):
                    group(part, gg, True)
            for gg in range(GROUPS):
                group(PARTS - 1, gg, False)

        def steps(part, gg, build):
            return group_steps(gg, build, not (isinstance(part, int) and part == 0 and gg == 0),
                               isinstance(part, int) and part == PARTS - 1 and gg == GROUPS - 1)

        def chunk(part, gg, c):
            q = CG * (GROUPS * part + gg) + c
            if c < 0:
                part, gg = before(part, gg)
            if c == CG:
                part, gg = (part, gg + 1) if gg < GROUPS - 1 else (part + 1, 0)
            return part, gg, c % CG, q

        def before(part, gg):
            return (part, gg - 1) if gg else (part - 1, GROUPS - 1)

        @block.sync
        def _(sp):
            sp.dma_start(iota_f[:], d.iota).then_inc(iota_in, 16)

            def load_u(part, gg, c):
                part, gg, c, q = chunk(part, gg, c)
                wait(sp, a_done, 2 * (q - 1))
                sp.dma_start(u[:, c % 2], d.uT[bass.ds(q, 1)].rearrange("o p k e -> (o p) k e")
                             ).then_inc(u_in[c % 2], 16)

            def load_v(part, gg, m):
                g = GROUPS * part + gg
                wait(sp, v_done, 2 * KT // VS * (VS * g + m - 1))
                sp.dma_start(vv[:, m % 2], d.v[:, bass.ds(g, 1), :, m * VC:(m + 1) * VC
                                               ].rearrange("p o c n -> p (o c) n")).then_inc(v_in[m % 2], 16)

            def group(part, gg, build):
                for what, *at in steps(part, gg, False):
                    if what == "u":
                        load_u(part, gg, *at)
                    if what == "w":
                        load_v(*before(part, gg), *at) if at[0] < VS else load_v(part, gg, 0)

            load_u(0, 0, 0)
            run_parts(sp, group)
            for m in range(1, VS):
                load_v(PARTS - 1, GROUPS - 1, m)

        @block.tensor
        def _(pe):
            def activate(part, gg, c, z):
                g = GROUPS * part + gg
                q = 2 * (CG * g + c) + z
                if z == 0:
                    pe.wait_ge(u_split, CG * g + c + 1)
                wait(pe, acted, q - 1)
                half = slice(z * HT, (z + 1) * HT)
                for k in range(KT):
                    for n, (x, y) in enumerate(((u_high, h_high), (u_high, h_low), (u_low, h_high))):
                        ins = pe.matmul(a_ps[z][:, 0:HT], x[:, c % 2, k], y[:, k, half],
                                        start=(k == 0 and n == 0), stop=(k == KT - 1 and n == 2))
                ins.then_inc(a_done, 1)

            def weigh(part, gg, m, z):
                g = GROUPS * part + gg
                q = 2 * (KT * g + m) + z
                of, at = m * P // VC, m * P % VC
                if at == 0 and z == 0:
                    pe.wait_ge(v_split, VS * g + of + 1)
                if m == 0 and z == 0:
                    pe.wait_ge(p_split, 2 * CG * (g + 1))
                wait(pe, y_added, q - 3)
                for c in range(CG):
                    high = slab(p_high, part % 2, CG * gg + c, z)
                    low = p_low[:, CG * (gg % 2) + c, z * HT:(z + 1) * HT]
                    for n, (x, y) in enumerate(((v_high, high), (v_high, low), (v_low, high))):
                        ins = pe.matmul(y_ps[(2 * m + z) % 4][:, 0:HT], x[:, of % 2, c, at:at + P], y,
                                        start=(c == 0 and n == 0), stop=(c == CG - 1 and n == 2))
                ins.then_inc(v_done, 1)

            def gates(part, n):
                m, w = BPP * part + n, unit_of[n]
                if unit_at[w] == n:
                    pe.wait_ge(w_ready, UPP * part + w + 1)
                pe.wait_ge(hot_ready, m + 1)
                wait(pe, built, m - 1)
                for t in range(TB):
                    out = g_ps[n % 2][:, t * 3 * CPP:(t + 1) * 3 * CPP].rearrange("p (w c) -> p w c", w=3)
                    ins = pe.matmul(out, hot[:, n % HOTS, :, t], wsec[:, w % 2, :, :, (n - unit_at[w]) * TB + t],
                                    start=True, stop=True)
                ins.then_inc(g_done, 1)

            for what, n in build_steps():
                if what == "b":
                    gates(0, n)
            pe.wait_ge(h_split, KT)

            def group(part, gg, build):
                for what, *at in steps(part, gg, build):
                    if what == "a":
                        activate(part, gg, *at)
                    if what == "v":
                        weigh(*before(part, gg), *at)
                    if what == "b":
                        gates(part + 1, *at)

            run_parts(pe, group)
            for m in range(KT):
                for z in range(2):
                    weigh(PARTS - 1, GROUPS - 1, m, z)

        @block.scalar
        def _(act):
            def round_u(part, gg, c):
                part, gg, c, q = chunk(part, gg, c)
                act.wait_ge(u_in[c % 2], 16 * (2 * (GROUPS * part + gg) + c // 2 + 1))
                nc.scalar.copy(u_high[:, c % 2], u[:, c % 2]).then_inc(u_rounded, 1)

            def round_v(part, gg, m):
                act.wait_ge(v_in[m % 2], 16 * (VS // 2 * (GROUPS * part + gg) + m // 2 + 1))
                nc.scalar.copy(v_high[:, m % 2], vv[:, m % 2]).then_inc(v_rounded, 1)

            def gelu(part, gg, c, z):
                q = 2 * (CG * (GROUPS * part + gg) + c) + z
                wait(act, p_split, q - 3)
                act.wait_ge(a_done, q + 1)
                nc.scalar.activation(gel[:, (2 * c + z) % 4], a_ps[z][:, 0:HT],
                                     ACT.Gelu_apprx_tanh).then_inc(acted, 1)

            def round_p(part, gg, c, z):
                part, gg, c, q = chunk(part, gg, c)
                act.wait_ge(gated, 2 * q + z + 1)
                nc.scalar.copy(slab(p_high, part % 2, CG * gg + c, z), gel[:, (2 * c + z) % 4]
                               ).then_inc(p_rounded, 1)

            def group(part, gg, build):
                for what, *at in steps(part, gg, False):
                    if what == "u":
                        round_u(part, gg, *at)
                    if what == "a":
                        gelu(part, gg, *at)
                    if what == "p":
                        round_p(part, gg, *at)
                    if what == "w":
                        round_v(*before(part, gg), *at) if at[0] < VS else round_v(part, gg, 0)

            for k in range(KT):
                nc.scalar.copy(h_high[:, k], h2T[:, k]).then_inc(h_rounded, 1)
            round_u(0, 0, 0)
            run_parts(act, group)
            round_p(PARTS - 1, GROUPS - 1, CG - 1, 1)
            for m in range(1, VS):
                round_v(PARTS - 1, GROUPS - 1, m)

        @block.gpsimd
        def _(pool):
            def low(part, whole, high, rounded, value):
                pool.wait_ge(rounded, value)
                return nc.gpsimd.tensor_tensor(part, whole, high.bitcast(F32), ALU.subtract)

            def split_u(part, gg, c):
                part, gg, c, q = chunk(part, gg, c)
                low(u_low[:, c % 2], u[:, c % 2], u_high[:, c % 2], u_rounded, q + 1).then_inc(u_split, 1)

            def split_v(part, gg, m):
                low(v_low[:, m % 2], vv[:, m % 2], v_high[:, m % 2], v_rounded,
                    VS * (GROUPS * part + gg) + m + 1).then_inc(v_split, 1)

            def split_p(part, gg, c, z):
                part, gg, c, q = chunk(part, gg, c)
                wait(pool, v_done, 2 * KT * (GROUPS * part + gg - 1))
                low(p_low[:, CG * (gg % 2) + c, z * HT:(z + 1) * HT], gel[:, (2 * c + z) % 4],
                    slab(p_high, part % 2, CG * gg + c, z), p_rounded, 2 * q + z + 1).then_inc(p_split, 1)

            def group(part, gg, build):
                for what, *at in steps(part, gg, False):
                    if what == "u":
                        split_u(part, gg, *at)
                    if what == "p":
                        split_p(part, gg, *at)
                    if what == "w":
                        split_v(*before(part, gg), *at) if at[0] < VS else split_v(part, gg, 0)

            for k in range(KT):
                low(h_low[:, k], h2T[:, k], h_high[:, k], h_rounded, k + 1).then_inc(h_split, 1)
            split_u(0, 0, 0)
            run_parts(pool, group)
            split_p(PARTS - 1, GROUPS - 1, CG - 1, 1)
            for m in range(1, VS):
                split_v(PARTS - 1, GROUPS - 1, m)

        @block.vector
        def _(dve):
            dve.wait_ge(iota_in, 16)
            nc.vector.memset(yT[:], 0.0)
            iota = iota_f[:].rearrange("p (k o) -> p k o", o=1)
            nc.vector.tensor_copy(count_c[:], spread(iota[:, 0:CPP], [P, CPP, UT_MAX]))
            nc.vector.tensor_copy(count_k[:], spread(iota, [P, NK, TB])).then_inc(consts, 1)

            def one_hots(part, n):
                wait(dve, g_done, BPP * part + n - (HOTS - 1))
                dve.wait_ge(consts, 1)
                key = e1T[:, n * TB:(n + 1) * TB].rearrange("p (o t) -> p o t", o=1)
                nc.vector.tensor_tensor(hot[:, n % HOTS], count_k[:], spread(key, [P, NK, TB]), ALU.is_equal
                                        ).then_inc(hot_ready, 1)

            def second(part, w):
                uw = UPP * part + w
                t0 = unit_at[w] * TB
                n = unit_of.count(w) * TB
                key = e2T[:, t0:t0 + n].rearrange("p (o t) -> p o t", o=1)
                if w == 0:
                    wait(dve, moved, part)
                wait(dve, w_ready, uw)
                dve.wait_ge(consts, 1)
                nc.vector.tensor_tensor(eq2[:, :, 0:n], count_c[:, :, 0:n], spread(key, [P, CPP, n]), ALU.is_equal
                                        ).then_inc(eq_ready, 1)
                wait(dve, g_done, BPP * part + (unit_at[w - 1] if w else unit_at[UPP - 1] - BPP))
                dve.wait_ge(eq_ready, uw + 1)
                for i in range(3):
                    wi = w3[:, i, t0:t0 + n].rearrange("p (o t) -> p o t", o=1)
                    ins = nc.vector.tensor_tensor(wsec[:, w % 2, i, :, 0:n], eq2[:, :, 0:n], spread(wi, [P, CPP, n]),
                                                  ALU.mult)
                ins.then_inc(w_ready, 1)
                if w == UPP - 1:
                    nc.vector.tensor_scalar(e2T[:], e2T[:], -float(CPP), None, ALU.add).then_inc(moved, 1)

            def take_gates(part, n):
                dve.wait_ge(g_done, BPP * part + n + 1)
                if n == 0:
                    wait(dve, v_done, 2 * KT * GROUPS * (part - 1))
                dve.wait_ge(consts, 1)
                src = g_ps[n % 2][:, 0:TB * 3 * CPP].rearrange("p (t w c) -> p t c w", t=TB, w=3)
                dst = gate[:, bass.ds(part % 2, 1), :, n * TB:(n + 1) * TB].rearrange("p o c t -> p t (o c)")
                nc.vector.tensor_reduce(dst, src, AX_X, ALU.add).then_inc(built, 1)

            def multiply(part, gg, c, z):
                q = 2 * (CG * (GROUPS * part + gg) + c) + z
                if gg == 0 and c == 0 and z == 0:
                    dve.wait_ge(built, BPP * (part + 1))
                dve.wait_ge(acted, q + 1)
                x = gel[:, (2 * c + z) % 4]
                nc.vector.tensor_tensor(x, x, slab(gate, part % 2, CG * gg + c, z), ALU.mult).then_inc(gated, 1)

            def add(part, gg, m, z):
                q = 2 * (KT * (GROUPS * part + gg) + m) + z
                wait(dve, y_added, q - 2 * KT + 1)
                dve.wait_ge(v_done, q + 1)
                acc = yT[:, m, z * HT:(z + 1) * HT]
                nc.vector.tensor_tensor(acc, acc, y_ps[(2 * m + z) % 4][:, 0:HT], ALU.add).then_inc(y_added, 1)

            def build(part, what, n):
                {"s": second, "h": one_hots, "b": take_gates}[what](part, n)

            for what, n in build_steps():
                build(0, what, n)

            def group(part, gg, do_build):
                for what, *at in steps(part, gg, do_build):
                    if what == "a":
                        multiply(part, gg, *at)
                    elif what == "v":
                        add(*before(part, gg), *at)
                    elif what in "shb":
                        build(part + 1, what, *at)

            run_parts(dve, group)
            for m in range(KT):
                for z in range(2):
                    add(PARTS - 1, GROUPS - 1, m, z)


def finish(nc, d, s):
    with ExitStack() as ctx:
        sb = lambda n, sh, dt=F32: ctx.enter_context(nc.sbuf_tensor(n, sh, dt))
        sem = lambda n: ctx.enter_context(nc.semaphore(n))
        x1 = sb("x1_back", [P, TILES, D])
        xo = sb("xo", [P, TILES, D])
        gf = sb("gf", [P, D])
        ss = sb("ss3", [P, TILES])
        rt = sb("rt3", [P, TILES])
        banks = [ctx.enter_context(nc.psum_tensor(f"f_ps{b}", [P, 512], F32)) for b in range(4)]
        x_in, g_in = sem("x_in"), sem("g_in")
        turned, added, squared, meaned = sem("turned"), sem("added"), sem("squared"), sem("meaned")
        rooted, inverted, scaled, done, stored = (sem(x) for x in ("rooted", "inverted", "scaled", "done", "stored"))
        block = ctx.enter_context(nc.Block())
        ident, yT = s.ident, s.yT

        @block.sync
        def _(sp):
            sp.dma_start(x1[:, 0:4], d.x1[0:SEQ].rearrange("(i p) n -> p i n", p=P)).then_inc(x_in, 16)
            sp.dma_start(x1[0:NS, 4], d.x1[SEQ:T]).then_inc(x_in, 16)
            sp.dma_start(gf[:], spread(d.gf, [P, D])).then_inc(g_in, 16)
            for i in range(TILES):
                sp.wait_ge(done, i + 1)
                sp.dma_start(d.out_y[i * P:i * P + ROWS[i]], xo[0:ROWS[i], i]).then_inc(stored, 16)
            sp.wait_ge(stored, 16 * TILES)

        @block.tensor
        def _(pe):
            for i in range(TILES):
                for n in range(2):
                    q = 2 * i + n
                    wait(pe, added, q - 3)
                    for j in range(4):
                        ins = pe.transpose(banks[q % 4][0:ROWS[i], j * P:(j + 1) * P], yT[:, 4 * n + j, cols(i)],
                                           ident[:])
                    ins.then_inc(turned, 1)

        @block.scalar
        def _(act):
            for i in range(TILES):
                r = ROWS[i]
                act.wait_ge(added, 2 * (i + 1))
                nc.scalar.activation(xo[0:r, i], x1[0:r, i], ACT.Square, accum_out=ss[0:r, i:i + 1]
                                     ).then_inc(squared, 1)
                act.wait_ge(meaned, i + 1)
                nc.scalar.activation(rt[0:r, i:i + 1], ss[0:r, i:i + 1], ACT.Sqrt).then_inc(rooted, 1)
                act.wait_ge(inverted, i + 1)
                nc.scalar.activation(xo[0:r, i], x1[0:r, i], ACT.Copy, scale=rt[0:r, i:i + 1]).then_inc(scaled, 1)

        @block.vector
        def _(dve):
            dve.wait_ge(x_in, 32)
            dve.wait_ge(g_in, 16)

            def gain(i):
                r = ROWS[i]
                dve.wait_ge(scaled, i + 1)
                nc.vector.tensor_tensor(xo[0:r, i], xo[0:r, i], gf[0:r], ALU.mult).then_inc(done, 1)

            for i in range(TILES):
                r = ROWS[i]
                for n in range(2):
                    q = 2 * i + n
                    dve.wait_ge(turned, q + 1)
                    half = x1[0:r, i, n * 512:(n + 1) * 512]
                    nc.vector.tensor_tensor(half, half, banks[q % 4][0:r], ALU.add).then_inc(added, 1)
                dve.wait_ge(squared, i + 1)
                nc.vector.tensor_scalar(ss[0:r, i:i + 1], ss[0:r, i:i + 1], 1.0 / D, RMS_EPS, ALU.mult, ALU.add
                                        ).then_inc(meaned, 1)
                dve.wait_ge(rooted, i + 1)
                nc.vector.reciprocal(rt[0:r, i:i + 1], rt[0:r, i:i + 1]).then_inc(inverted, 1)
                if i:
                    gain(i - 1)
            gain(TILES - 1)


class Names(dict):

    def __getattr__(self, name):
        return self[name]


def build(nc, d):
    with ExitStack() as ctx:
        def kept(stack, name, shape, dt=F32):
            return stack.enter_context(nc.sbuf_tensor(name, shape, dt))

        s = Names()
        s["ident"] = kept(ctx, "ident", [P, P])
        s["catT"] = s["yT"] = kept(ctx, "catT_then_yT", [P, KT, T])
        with ExitStack() as first:
            s["qT"] = kept(first, "qT", [P, PAIRS, T])
            s["kT"] = kept(first, "kT", [P, PAIRS, T])
            s["v"] = kept(first, "v", [P, TILES, AW])
            s["gp"] = kept(first, "gp", [P, 2, TAPS - 1 + SEQ])
            s["gs"] = kept(first, "gs", [P, 2, DEC_B, TAPS - 1 + DEC_T])
            project(nc, d, s)
            mix(nc, d, s)
        s["h2T"], s["h_low"] = over(nc, ctx, "h2T", "h_low", [P, KT, T])
        s["e1T"] = kept(ctx, "e1T", [P, T], BF16)
        s["e2T"] = kept(ctx, "e2T", [P, T], BF16)
        s["w3"] = kept(ctx, "w3", [P, 3, T], BF16)
        choose(nc, d, s)
        experts(nc, d, s)
        finish(nc, d, s)


def kernel(x_prompt, x_sample, cache_k, cache_v, state_conv, norm1_g, w_in, conv_w, conv_b,
           conv_ln_g, conv_ln_b, w_out, norm2_g, w_query, sub_keys1, sub_keys2,
           expert_u, expert_v, final_g):
    import concourse.bacc as bacc
    from concourse.bass_utils import run_bass_kernel_spmd

    f = lambda a: np.asarray(a)
    c = np.ascontiguousarray
    cos, sin = rope_tables()
    x = np.concatenate([f(x_prompt).reshape(SEQ, D), f(x_sample).reshape(NS, D)])
    given = {
        "x": x,
        "xT": c(x.T.reshape(KT, P, T).transpose(1, 0, 2)),
        "g1": c(f(norm1_g).reshape(KT, P).T),
        "w_in": c(f(w_in)[0].reshape(KT, P, NCB, CB).transpose(2, 1, 0, 3)),
        "cos": cos,
        "sin": sin,
        "ident": np.eye(P, dtype=np.float32),
        "state": c(f(state_conv)[0].transpose(2, 0, 1).reshape(2, P, DEC_B, TAPS - 1).transpose(1, 0, 2, 3)),
        "state_rows": c(f(state_conv)[0]),
        "ckT": c(f(cache_k)[0].reshape(DEC_B, PAST, PAIRS, P).transpose(0, 3, 2, 1)),
        "cv": c(f(cache_v)[0].reshape(DEC_B, 2, P, AW).transpose(0, 2, 1, 3)),
        "pmask": prompt_mask(),
        "smask": sample_mask(),
        "conv_w": c(f(conv_w)[0].T.reshape(2, P, TAPS).transpose(1, 0, 2)),
        "conv_b": c(f(conv_b)[0].reshape(2, P).T),
        "ln_g": c(f(conv_ln_g)[0].reshape(1, CH)),
        "ln_b": c(f(conv_ln_b)[0].reshape(1, CH)),
        "w_out": c(f(w_out)[0].reshape(KT, P, D).transpose(1, 0, 2)),
        "g2": c(f(norm2_g)[0].reshape(KT, P).T),
        "w_q": c(f(w_query)[0].reshape(KT, P, 2 * PH, P).transpose(2, 1, 0, 3)),
        "keysT": c(np.stack([f(sub_keys1)[0].T, f(sub_keys2)[0].T], 1)),
        "uT": c(f(expert_u)[0].reshape(NK, NK, KT, P).transpose(1, 3, 2, 0)),
        "v": c(f(expert_v)[0].reshape(NK, NG, CG, D)),
        "gf": c(f(final_g).reshape(1, D)),
        "iota": np.tile(np.arange(NK, dtype=np.float32), (P, 1)),
    }
    outs = {
        "out_y": (T, D),
        "out_k": (T, AW),
        "out_v": (T, AW),
        "out_cp": (TAPS - 1, CH),
        "out_cs": (DEC_B, TAPS - 1, CH),
    }
    nc = bacc.Bacc("TRN2", target_bir_lowering=False, num_devices=1)
    d = Names()
    for name, a in given.items():
        d[name] = nc.dram_tensor(f"in_{name}", a.shape, F32, kind="ExternalInput").ap()
    for name, shape in outs.items():
        d[name] = nc.dram_tensor(name, shape, F32, kind="ExternalOutput").ap()
    d["x1"] = nc.dram_tensor("x1_kept", (T, D), F32, kind="Internal").ap()
    build(nc, d)
    r = run_bass_kernel_spmd(nc, [{f"in_{n}": a for n, a in given.items()}], core_ids=[0]).results[0]
    y, k, v = r["out_y"], r["out_k"], r["out_v"]
    heads = lambda a, b, t: a.reshape(1, b, t, NH, HD)
    return (y[:SEQ].reshape(1, SEQ, D), y[SEQ:].reshape(DEC_B, DEC_T, D),
            heads(k[:SEQ], 1, SEQ), heads(v[:SEQ], 1, SEQ), r["out_cp"].reshape(1, 1, TAPS - 1, CH),
            heads(k[SEQ:], DEC_B, DEC_T), heads(v[SEQ:], DEC_B, DEC_T),
            r["out_cs"].reshape(1, DEC_B, TAPS - 1, CH))
```

```python
from contextlib import ExitStack

import numpy as np

import concourse.bass as bass
from concourse import mybir

F32 = mybir.dt.float32
F32R = mybir.dt.float32r
BF16 = mybir.dt.bfloat16
U32 = mybir.dt.uint32
ALU = mybir.AluOpType
ACT = mybir.ActivationFunctionType
AX_X = mybir.AxisListType.X

P = 128
D = 1024
KT = D // P
SEQ = 512
DEC_B, DEC_T = 8, 4
NS = DEC_B * DEC_T
T = SEQ + NS
HT = T // 2
TILES = 5
ROWS = [P] * 4 + [NS]
HD, NH = 64, 12
AW = NH * HD
PAIRS = NH // 2
CH = D - AW
TAPS = 31
PAST = 256
CB = 256
NCB = (3 * AW + 2 * CH) // CB
NSK = PAST + NS
SROWS = NH * DEC_T
NEG = -1.0e30
SCALE = HD ** -0.5
RMS_EPS, LN_EPS = 1e-6, 1e-5
DILATIONS = ((128, 1), (512, 4), (2048, 16))
PH, TOPK, NK = 8, 16, 128
SLOTS = PH * TOPK
HT8 = TOPK // 2
TAIL = TOPK + (HT8 - 1) * HT8
SUMS = TAIL + HT8
CPP = 16
PARTS = NK // CPP
CG = 4
GROUPS = CPP // CG
NG = PARTS * GROUPS
TB = 8
DT = T - P
BPP = DT // TB
UNITS = ((2, 2), (4, 4, 4, 4), (4, 4, 4, 4), (4, 4, 4, 4))
UPP = sum(len(g) for g in UNITS)
UT_MAX = max(max(g) for g in UNITS) * TB
HOTS = 4
FIRST_A, FIRST_K = [BPP // 4 + 2 * n for n in range(16)], CG * KT // 16
assert FIRST_A[-1] < BPP
WO_AT = 229344 - KT * D * 4
LEAD = 2
VS = 4
VC = D // VS
PPH = PARTS // 2
FPP = SLOTS // PPH
FPG = FPP // GROUPS
ROW_BUFS = 4
assert FPP % ROW_BUFS == 0
assert sum(map(sum, UNITS)) == BPP and UPP % 2 == 0 and BPP % HOTS == 0


def group_steps(gg, build, weigh, last=False, fetch=None):
    heavy = []
    for c in range(CG):
        if weigh:
            heavy.append(("p", c - 1))
        if not (last and c == CG - 1):
            heavy.append(("u", c + 1))
        heavy.append(("a", c))
        if weigh:
            lo, hi = (c, c + 1) if gg else (2 * c, 2 * c + 2) if c < 2 else (VS, VS)
            for m in range(lo, hi):
                heavy.append(("w", m + 1))
                heavy += [("v", m * KT // VS + k) for k in range(KT // VS)]
    if not weigh:
        heavy += [("p", c) for c in range(CG)] + [("w", VS)]
    if fetch is not None:
        tasks = [i for i, x in enumerate(heavy) if x[0] in ("av" if weigh else "w")][weigh and gg == 0:]
        for j in reversed(range(FPG)):
            heavy.insert(tasks[j * len(tasks) // FPG] + 1, ("d", FPG * gg + j))
        if gg == 0:
            heavy.insert([x[0] for x in heavy].index("a" if weigh else "d"), ("i",))
        if gg == GROUPS - 1 and fetch == 0:
            heavy.append(("c",))
    if not build:
        return heavy
    cost = {"a": 2, "v": 1}
    skip = 0 if gg else 1 + max([i for i, x in enumerate(heavy) if x[0] == "v"], default=1)
    total = sum(cost.get(x[0], 0) for x in heavy[skip:])
    n, w = sum(map(sum, UNITS[:gg])), sum(map(len, UNITS[:gg]))
    count = sum(UNITS[gg])
    starts = {n + sum(UNITS[gg][:k]): w + k for k in range(len(UNITS[gg]))}
    out, at, led, done = [], 0, 0, 0

    def lead(upto):
        nonlocal led
        while led < min(upto, count):
            if n + led in starts:
                out.append(("s", starts[n + led]))
            out.append(("h", n + led))
            led += 1

    for i, step in enumerate(heavy):
        now = 0
        if i >= skip:
            at += cost.get(step[0], 0)
            now = max(0, -(-count * at // total) - done)
            if now:
                lead(done + now + LEAD)
        elif step[0] in "av":
            lead(LEAD)
        out.append(step)
        out += [("b", done + n + k) for k in range(now)]
        done += now
    assert done == count and led == count
    return out


def build_steps():
    out = []
    for gg in range(GROUPS):
        out += [x for x in group_steps(gg, True, False) if x[0] in "shb"]
    return out


def rope_tables():
    half = HD // 2
    inv = np.power(np.float32(10000.0), -np.arange(half, dtype=np.float32) * np.float32(2.0 / HD))
    pos = np.zeros((TILES, P), np.float32)
    pos[:4] = np.arange(SEQ, dtype=np.float32).reshape(4, P)
    pos[4, :NS] = PAST + np.tile(np.arange(DEC_T, dtype=np.float32), DEC_B)
    ang = (pos[:, :, None] * inv.astype(np.float32)).astype(np.float32)
    cos, sin = np.cos(ang).astype(np.float32), np.sin(ang).astype(np.float32)
    cos = np.concatenate([cos, cos], -1).transpose(1, 0, 2)
    sin = np.concatenate([-sin, sin], -1).transpose(1, 0, 2)
    return np.ascontiguousarray(cos), np.ascontiguousarray(sin)


def reach_count(dist):
    n = np.zeros(dist.shape, np.float64)
    for win, dil in DILATIONS:
        n += (dist >= 0) & (dist % dil == 0) & (dist // dil <= win // dil)
    return n


def added_mask(count):
    return np.where(count > 0, np.log(np.maximum(count, 1)) / SCALE, NEG).astype(np.float32)


def prompt_mask():
    t = np.arange(SEQ)
    m = added_mask(reach_count(t[:, None] - t[None, :]))
    return np.ascontiguousarray(m.reshape(4, P, SEQ).transpose(1, 0, 2))


def sample_mask():
    i = np.arange(DEC_T)
    cached = added_mask(reach_count(PAST + i[:, None] - np.arange(PAST)[None, :]))
    m = np.full((NH, DEC_T, DEC_B, NSK), NEG, np.float32)
    m[:, :, :, :PAST] = cached[None, :, None, :]
    new = added_mask(reach_count(i[:, None] - i[None, :]))
    for b in range(DEC_B):
        m[:, :, b, PAST + b * DEC_T:PAST + (b + 1) * DEC_T] = new[None]
    return np.ascontiguousarray(m.reshape(SROWS, DEC_B, NSK))


def cols(i):
    return slice(i * P, i * P + ROWS[i])


def spread(ap, shape):
    return ap.to_broadcast(shape)


def project(nc, d, s):
    with ExitStack() as ctx:
        sb = lambda n, sh, dt=F32: ctx.enter_context(nc.sbuf_tensor(n, sh, dt))
        sem = lambda n: ctx.enter_context(nc.semaphore(n))
        w = sb("w_in_sb", [P, NCB, KT, CB])
        xT = sb("xT", [P, KT, T])
        xtok = sb("xtok", [P, 2, D])
        sq = sb("sq", [P, D])
        g1 = sb("g1", [P, KT])
        ss = sb("ss", [P, TILES])
        rstd = sb("rstd1", [P, TILES])
        cos = sb("cos", [P, TILES, HD])
        sin = sb("sin", [P, TILES, HD])
        qk = sb("qk", [P, 2 * AW])
        rot = sb("rot", [P, 2 * AW])
        qkr = sb("qkr", [P, 2 * AW])
        u1 = sb("u1", [P, CH])
        sg = sb("sg", [P, CH])
        g = sb("g", [P, CH])
        proj_ps = [ctx.enter_context(nc.psum_tensor(f"proj{b}", [P, 512], F32)) for b in range(4)]
        turn_ps = [ctx.enter_context(nc.psum_tensor(f"turn{b}", [P, 512], F32)) for b in range(4)]

        ident_in = sem("ident_in")
        x0_in, x_in, tab_in, hist_in = sem("x0_in"), sem("x_in"), sem("tab_in"), sem("hist_in")
        w_sets = ((0, 1), (1, 2), (2, 3), (3, 5), (5, 7), (7, 9), (9, NCB))
        w_loaded = [sem(f"w_in{a}") for a, _ in w_sets]
        squared, meaned, rooted, rstd_ready = sem("squared"), sem("meaned"), sem("rooted"), sem("rstd_ready")
        xg_ready = sem("xg_ready")
        xtok_in = [sem(f"xtok_in{b}") for b in range(2)]
        block_done, evacuated = sem("block_done"), sem("evacuated")
        rot_ready, cos_ready, roped = sem("rot_ready"), sem("cos_ready"), sem("roped")
        g_ready = sem("g_ready")
        turned, turn_read = sem("turned"), sem("turn_read")
        kept_stored, k_stored, v_stored, g_stored = (sem(x + "_stored") for x in ("kept", "k", "v", "g"))
        ss_set = sem("ss_set")
        block = ctx.enter_context(nc.Block())
        NQK = 2 * AW // CB
        ident, qT, kT, v, gp, gs = s.ident, s.qT, s.kT, s.v, s.gp, s.gs

        @block.sync
        def _(sp):
            sp.dma_start(g1[:], d.g1).then_inc(tab_in, 16)
            sp.dma_start(xT[:, :, cols(0)], d.xT[:, :, cols(0)]).then_inc(x0_in, 16)
            for n, (a, b) in enumerate(w_sets):
                sp.dma_start(w[:, a:b], d.w_in[a:b].rearrange("n p k c -> p n k c")).then_inc(w_loaded[n], 16)
                if n == 1:
                    sp.dma_start(xT[:, :, P:T], d.xT[:, :, P:T]).then_inc(x_in, 16)
            sp.dma_start(gs[:, :, :, 0:TAPS - 1], d.state).then_inc(hist_in, 16)
            sp.dma_start(d.out_cs[:, 0:TAPS - 1 - DEC_T], d.state_rows[:, DEC_T:TAPS - 1]).then_inc(kept_stored, 16)
            for i in range(TILES):
                r = ROWS[i]
                sp.wait_ge(roped, i + 1)
                sp.dma_start(d.out_k[i * P:i * P + r], qkr[0:r, AW:]).then_inc(k_stored, 16)
                sp.wait_ge(evacuated, NCB * i + 9)
                sp.dma_start(d.out_v[i * P:i * P + r], v[0:r, i]).then_inc(v_stored, 16)
                if i >= 3:
                    sp.wait_ge(g_ready, i + 1)
                    if i == 3:
                        sp.dma_start(d.out_cp, g[P - (TAPS - 1):P]).then_inc(g_stored, 16)
                    else:
                        sp.dma_start(d.out_cs[:, TAPS - 1 - DEC_T:], g[0:NS]).then_inc(g_stored, 16)
            sp.wait_ge(kept_stored, 16)
            sp.wait_ge(k_stored, 16 * TILES)
            sp.wait_ge(v_stored, 16 * TILES)
            sp.wait_ge(g_stored, 32)
            sp.wait_ge(hist_in, 16)

        @block.scalar
        def _(act):
            act.dma_start(xtok[:, 0], d.x[0:P]).then_inc(xtok_in[0], 16)
            act.dma_start(xtok[:, 1], d.x[P:2 * P]).then_inc(xtok_in[1], 16)
            act.dma_start(cos[:], d.cos).then_inc(tab_in, 16)
            act.dma_start(sin[:], d.sin).then_inc(tab_in, 16)
            act.dma_start(ident[:], d.ident).then_inc(ident_in, 16)
            act.wait_ge(ss_set, 1)

            def square(i):
                r = ROWS[i]
                act.wait_ge(xtok_in[i % 2], 16 * (i // 2 + 1))
                if i:
                    act.wait_ge(squared, i)
                nc.scalar.activation(sq[0:r], xtok[0:r, i % 2], ACT.Square,
                                     accum_out=ss[0:r, i:i + 1]).then_inc(squared, 1)
                if i + 2 < TILES:
                    act.wait_ge(squared, i + 1)
                    act.dma_start(xtok[0:ROWS[i + 2], i % 2],
                                  d.x[(i + 2) * P:(i + 2) * P + ROWS[i + 2]]).then_inc(xtok_in[i % 2], 16)

            def root(i):
                act.wait_ge(meaned, i + 1)
                nc.scalar.activation(rstd[:, i:i + 1], ss[:, i:i + 1], ACT.Sqrt).then_inc(rooted, 1)

            square(0)
            square(1)
            root(0)
            root(1)
            for i in range(TILES):
                r = ROWS[i]
                act.wait_ge(rstd_ready, i + 1)
                for n in range(NCB):
                    u = NCB * i + n
                    act.wait_ge(block_done, u + 1)
                    src = proj_ps[u % 4][0:r, 0:CB]
                    sc = rstd[0:r, i:i + 1]
                    if n < NQK:
                        if n == 0 and i:
                            act.wait_ge(cos_ready, i)
                        dst = qk[0:r, n * CB:(n + 1) * CB]
                    elif n < 9:
                        dst = v[0:r, i, (n - NQK) * CB:(n - NQK + 1) * CB]
                    else:
                        if n == 9 and i:
                            act.wait_ge(g_ready, i)
                        dst = (u1 if n == 9 else sg)[0:r]
                    f = ACT.Sigmoid if n == 10 else ACT.Copy
                    nc.scalar.activation(dst, src, f, scale=sc).then_inc(evacuated, 1)
                    if n == 6 and 2 <= i + 1 < TILES:
                        root(i + 1)
                if i + 2 < TILES:
                    square(i + 2)

        @block.vector
        def _(dve):
            nc.vector.memset(gp[:, :, 0:TAPS - 1], 0.0)
            nc.vector.memset(ss[:], 1.0).then_inc(ss_set, 1)
            dve.wait_ge(tab_in, 48)
            dve.wait_ge(x0_in, 16)

            def scale_x(a, b):
                nc.vector.tensor_tensor(xT[:, :, a:b], xT[:, :, a:b],
                                        spread(g1[:].rearrange("p (k o) -> p k o", o=1), [P, KT, b - a]),
                                        ALU.mult).then_inc(xg_ready, 1)

            scale_x(0, P)

            def mean(i):
                dve.wait_ge(squared, i + 1)
                x = ss[:, i:i + 1]
                nc.vector.tensor_scalar(x, x, 1.0 / D, RMS_EPS, ALU.mult, ALU.add).then_inc(meaned, 1)

            def invert(i):
                dve.wait_ge(rooted, i + 1)
                nc.vector.reciprocal(rstd[:, i:i + 1], rstd[:, i:i + 1]).then_inc(rstd_ready, 1)

            mean(0)
            mean(1)
            invert(0)
            invert(1)
            dve.wait_ge(x_in, 16)
            scale_x(P, T)

            def rope(i):
                r = ROWS[i]
                x4 = qk[0:r].rearrange("p (h s e) -> p h s e", s=2, e=HD // 2)
                o4 = rot[0:r].rearrange("p (h s e) -> p h s e", s=2, e=HD // 2)
                n = 2 * NH
                dve.wait_ge(evacuated, NCB * i + NQK)
                if i:
                    dve.wait_ge(roped, i)
                for half in range(2):
                    sn = sin[0:r, i, half * 32:half * 32 + 32].rearrange("p (o e) -> p o e", o=1)
                    nc.vector.tensor_tensor(o4[:, :, half], x4[:, :, 1 - half], spread(sn, [r, n, HD // 2]),
                                            ALU.mult).then_inc(rot_ready, 1)
                if i:
                    dve.wait_ge(turned, 4 * i)
                    dve.wait_ge(k_stored, 16 * i)
                cs = cos[0:r, i].rearrange("p (o e) -> p o e", o=1)
                nc.vector.tensor_tensor(qkr[0:r].rearrange("p (h e) -> p h e", e=HD),
                                        qk[0:r].rearrange("p (h e) -> p h e", e=HD),
                                        spread(cs, [r, n, HD]), ALU.mult).then_inc(cos_ready, 1)
                dve.wait_ge(cos_ready, i + 1)
                dve.wait_ge(rot_ready, 2 * (i + 1))
                nc.vector.tensor_tensor(qkr[0:r], qkr[0:r], rot[0:r], ALU.add).then_inc(roped, 1)
                dve.wait_ge(evacuated, NCB * (i + 1))
                if i == 4:
                    dve.wait_ge(g_stored, 16)
                nc.vector.tensor_tensor(g[0:r], u1[0:r], sg[0:r], ALU.mult).then_inc(g_ready, 1)

            def take(i):
                r = ROWS[i]
                for b in range(4):
                    dve.wait_ge(turned, 4 * i + b + 1)
                    src = turn_ps[b][:, 0:4 * r].rearrange("p (j t) -> p j t", t=r)
                    if b < 3:
                        for j in range(4):
                            m = 4 * b + j
                            dst = (qT if m < PAIRS else kT)[:, m % PAIRS, cols(i)]
                            ins = nc.vector.tensor_copy(dst, src[:, j])
                    elif i < 4:
                        ins = nc.vector.tensor_copy(gp[:, :, TAPS - 1 + i * P:TAPS - 1 + (i + 1) * P], src[:, 0:2])
                    else:
                        ins = nc.vector.tensor_copy(gs[:, :, :, TAPS - 1:],
                                                    src[:, 0:2].rearrange("p c (b t) -> p c b t", t=DEC_T))
                    ins.then_inc(turn_read, 1)

            for i in range(TILES):
                rope(i)
                if i + 2 < TILES:
                    mean(i + 2)
                    invert(i + 2)
                take(i)

        @block.tensor
        def _(pe):
            def turn(i):
                r = ROWS[i]
                if i == 0:
                    pe.wait_ge(ident_in, 16)
                for b in range(4):
                    if b == 0:
                        pe.wait_ge(roped, i + 1)
                    if b == 3:
                        pe.wait_ge(g_ready, i + 1)
                    if i:
                        pe.wait_ge(turn_read, 4 * (i - 1) + b + 1)
                    for j in range(4 if b < 3 else 2):
                        src = qkr[0:r, (4 * b + j) * P:(4 * b + j + 1) * P] if b < 3 else g[0:r, j * P:(j + 1) * P]
                        ins = pe.transpose(turn_ps[b][:, j * r:(j + 1) * r], src, ident[0:r, 0:r])
                    ins.then_inc(turned, 1)

            for i in range(TILES):
                pe.wait_ge(xg_ready, 1 if i == 0 else 2)
                for n in range(NCB):
                    u = NCB * i + n
                    if i == 0:
                        pe.wait_ge(w_loaded[[a <= n < b for a, b in w_sets].index(True)], 16)
                    if u >= 4:
                        pe.wait_ge(evacuated, u - 3)
                    for k in range(KT):
                        ins = pe.matmul(proj_ps[u % 4][0:ROWS[i], 0:CB], xT[:, k, cols(i)], w[:, n, k],
                                        start=(k == 0), stop=(k == KT - 1))
                    ins.then_inc(block_done, 1)
                    if n == 5 and i:
                        turn(i - 1)
            turn(TILES - 1)


def mix(nc, d, s):
    units = [(i, h) for i in range(4) for h in range(NH)] + [(4, b) for b in range(DEC_B)]
    U = len(units)
    UP = 4 * NH
    CATS = [NH * (i + 1) + 4 + n for i in range(4) for n in range(2)]
    Y_TURNS = [43, 44, 45]
    CAT_BEFORE_Y = sum(t < Y_TURNS[0] for t in CATS)
    NORM_AT = 46
    BACK = [54, 55, 56]
    RING, V_RING = 3, 4

    def keys(u):
        return (units[u][0] + 1) * P if u < UP else NSK

    def rows(u):
        return P if u < UP else SROWS

    with ExitStack() as ctx:
        sb = lambda n, sh, dt=F32: ctx.enter_context(nc.sbuf_tensor(n, sh, dt))
        sem = lambda n: ctx.enter_context(nc.semaphore(n))
        pmask = sb("pmask", [P, 4, SEQ])
        smask = sb("smask", [SROWS, DEC_B, NSK])
        ckT = sb("ckT", [P, RING, PAIRS, PAST])
        cv = sb("cv", [P, V_RING, 2, AW])
        qbd = sb("qbd", [P, DEC_B, PAIRS, SROWS])
        sm = sb("sm", [P, 3, SEQ])
        pr = sb("pr", [P, 3, SEQ])
        prT = sb("prT", [P, 3, SEQ])
        mx = sb("mx", [P, U])
        nmx = sb("nmx", [P, U])
        den = sb("den", [P, U])
        rden = sb("rden", [P, U])
        attn = sb("attn", [P, 2, AW])
        cw = sb("cw", [P, 2, TAPS])
        cb = sb("cb", [P, 2])
        lng = sb("lng", [P, CH])
        lnb = sb("lnb", [P, CH])
        y = sb("y", [P, 2, T])
        yt = sb("yt", [P, TILES, CH])
        yn = sb("yn", [P, TILES, CH])
        ysig = yt
        st = sb("st", [P, TILES, 6])
        mv = sb("mv", [P, TILES, 2])
        lr = sb("lr", [P, TILES])
        s_ps = [ctx.enter_context(nc.psum_tensor(f"s_ps{b}", [P, 512], F32)) for b in range(3)]
        t_ps = [ctx.enter_context(nc.psum_tensor(f"t_ps{b}", [P, 512], F32)) for b in range(2)]
        o_ps = [ctx.enter_context(nc.psum_tensor(f"o_ps{b}", [P, 512], F32)) for b in range(2)]
        c_ps = ctx.enter_context(nc.psum_tensor("c_ps", [P, 512], F32))
        assert nc.sbuf_base <= WO_AT, nc.sbuf_base - WO_AT

        mask_in, conv_in, ln_in = sem("mask_in"), sem("conv_in"), sem("ln_in")
        ck_in = [sem(f"ck_in{b}") for b in range(RING)]
        cv_in = [sem(f"cv_in{b}") for b in range(V_RING)]
        qbd_zero, qbd_ready = sem("qbd_zero"), sem("qbd_ready")
        scored, maxed, neg_ready, exped = sem("scored"), sem("maxed"), sem("neg_ready"), sem("exped")
        rden_ready, scaled = sem("rden_ready"), sem("scaled")
        turned, copied, summed, normed = sem("turned"), sem("copied"), sem("summed"), sem("normed")
        cat_turned, cat_taken = sem("cat_turned"), sem("cat_taken")
        tapped = sem("tapped")
        y_turned, y_taken, stats, aggr, eps_added = sem("y_turned"), sem("y_taken"), sem("stats"), sem("aggr"), sem("eps_added")
        rooted, lr_ready, centred = sem("rooted"), sem("lr_ready"), sem("centred")
        sig_ready, gated = sem("sig_ready"), sem("gated")
        g_turned, g_taken = sem("g_turned"), sem("g_taken")
        block = ctx.enter_context(nc.Block())
        ident, qT, kT, v, gp, gs, catT = s.ident, s.qT, s.kT, s.v, s.gp, s.gs, s.catT

        @block.sync
        def _(sp):
            sp.dma_start(pmask[:], d.pmask).then_inc(mask_in, 16)
            sp.dma_start(smask[:], d.smask).then_inc(mask_in, 16)
            sp.dma_start(cw[:], d.conv_w).then_inc(conv_in, 16)
            sp.dma_start(cb[:], d.conv_b).then_inc(conv_in, 16)
            sp.dma_start(lng[:], spread(d.ln_g, [P, CH])).then_inc(ln_in, 16)
            sp.dma_start(lnb[:], spread(d.ln_b, [P, CH])).then_inc(ln_in, 16)
            sp.dma_start(s.wo[:], d.w_out).then_inc(s.wo_in, 16)
            for b in range(DEC_B):
                if b >= RING:
                    sp.wait_ge(scored, UP + b - RING + 1)
                sp.dma_start(ckT[:, b % RING], d.ckT[b]).then_inc(ck_in[b % RING], 16)
                if b >= V_RING:
                    sp.wait_ge(summed, UP + b - V_RING + 1)
                sp.dma_start(cv[:, b % V_RING], d.cv[b]).then_inc(cv_in[b % V_RING], 16)

        @block.gpsimd
        def _(pool):
            nc.gpsimd.memset(qbd[:], 0.0).then_inc(qbd_zero, 1)
            pool.wait_ge(qbd_zero, 1)
            for j in range(PAIRS):
                for hh in range(2):
                    a, r0 = 64 * hh, 8 * j + 4 * hh
                    nc.gpsimd.tensor_copy(qbd[a:a + 64, :, j, r0:r0 + DEC_T],
                                          qT[a:a + 64, j, SEQ:T].rearrange("p (b t) -> p b t", t=DEC_T)
                                          ).then_inc(qbd_ready, 1)

        @block.tensor
        def _(pe):
            def score(u):
                i, h = units[u]
                if u >= 3:
                    pe.wait_ge(maxed, u - 2)
                n = keys(u)
                if u < UP:
                    a = 64 * (h % 2)
                    ins = pe.matmul(s_ps[u % 3][:, 0:n], qT[a:a + 64, h // 2, cols(i)], kT[a:a + 64, h // 2, 0:n],
                                    start=True, stop=True)
                else:
                    if u == UP:
                        pe.wait_ge(qbd_ready, 2 * PAIRS)
                    pe.wait_ge(ck_in[h % RING], 16 * (h // RING + 1))
                    for lo, hi in ((0, PAST), (PAST, NSK)):
                        for j in range(PAIRS):
                            rhs = ckT[:, h % RING, j] if lo == 0 else kT[:, j, SEQ:T]
                            ins = pe.matmul(s_ps[u % 3][0:SROWS, lo:hi], qbd[:, h, j], rhs,
                                            start=(j == 0), stop=(j == PAIRS - 1))
                ins.then_inc(scored, 1)

            def turn(u):
                if u < UP:
                    pe.wait_ge(exped, u + 1)
                else:
                    pe.wait_ge(scaled, u - UP + 1)
                if u >= 2:
                    pe.wait_ge(copied, u - 1)
                r, n = rows(u), keys(u)
                for q in range(0, n, P):
                    m = min(P, n - q)
                    c = q // P * r
                    ins = pe.transpose(t_ps[u % 2][0:m, c:c + r], pr[0:r, u % 3, q:q + m], ident[0:r, 0:r])
                ins.then_inc(turned, 1)

            def weigh(u):
                i, h = units[u]
                pe.wait_ge(copied, u + 1)
                if u >= 2:
                    pe.wait_ge(normed, u - 1)
                if u < UP:
                    for q in range(i + 1):
                        ins = pe.matmul(o_ps[u % 2][:, 0:HD], prT[:, u % 3, q * P:(q + 1) * P],
                                        v[:, q, h * HD:(h + 1) * HD], start=(q == 0), stop=(q == i))
                else:
                    pe.wait_ge(cv_in[h % V_RING], 16 * (h // V_RING + 1))
                    for j in range(PAIRS):
                        for q in range(3):
                            m = P if q < 2 else NS
                            val = cv[:, h % V_RING, q, j * P:(j + 1) * P] if q < 2 else v[0:NS, 4, j * P:(j + 1) * P]
                            c = q * SROWS + 8 * j
                            ins = pe.matmul(o_ps[u % 2][:, 8 * j:8 * j + 8], val, prT[0:m, u % 3, c:c + 8],
                                            start=(q == 0), stop=(q == 2))
                ins.then_inc(summed, 1)

            def turn_cat(i, b):
                pe.wait_ge(normed, NH * (i + 1))
                if 2 * i + b:
                    pe.wait_ge(cat_taken, 2 * i + b)
                for j in range(4 * b, min(4 * b + 4, PAIRS)):
                    ins = pe.transpose(c_ps[:, (j - 4 * b) * P:(j - 4 * b + 1) * P], attn[:, i % 2, j * P:(j + 1) * P],
                                       ident[:])
                ins.then_inc(cat_turned, 1)

            def turn_y(n):
                pe.wait_ge(tapped, 4 * TAPS)
                pe.wait_ge(cat_taken, CAT_BEFORE_Y)
                if n:
                    pe.wait_ge(y_taken, n)
                for i in range(2 * n, min(2 * n + 2, TILES)):
                    for c in range(2):
                        at = (i % 2) * CH + c * P
                        ins = pe.transpose(c_ps[0:ROWS[i], at:at + P], y[:, c, cols(i)], ident[:])
                ins.then_inc(y_turned, 1)

            def turn_back(n):
                pe.wait_ge(gated, min(2 * n + 2, TILES))
                pe.wait_ge(cat_taken, 8)
                if n:
                    pe.wait_ge(g_taken, n)
                for i in range(2 * n, min(2 * n + 2, TILES)):
                    r = ROWS[i]
                    for c in range(2):
                        at = (i % 2) * CH + c * r
                        ins = pe.transpose(c_ps[:, at:at + r], yn[0:r, i, c * P:(c + 1) * P], ident[0:r, 0:r])
                ins.then_inc(g_turned, 1)

            for t in range(U + 3):
                if t < U:
                    score(t)
                if 0 <= t - 2 < U:
                    turn(t - 2)
                if 0 <= t - 3 < U:
                    weigh(t - 3)
                if t in CATS:
                    if t == CATS[6]:
                        pe.wait_ge(y_taken, 3)
                    turn_cat(CATS.index(t) // 2, CATS.index(t) % 2)
                if t in Y_TURNS:
                    turn_y(Y_TURNS.index(t))
                if t in BACK:
                    turn_back(BACK.index(t))

        @block.scalar
        def _(act):
            def exp(u):
                r, n = rows(u), keys(u)
                act.wait_ge(neg_ready, u + 1)
                if u >= 3:
                    act.wait_ge(turned, u - 2)
                nc.scalar.activation(pr[0:r, u % 3, 0:n], sm[0:r, u % 3, 0:n], ACT.Exp, bias=nmx[0:r, u:u + 1],
                                     scale=SCALE, accum_out=den[0:r, u:u + 1]).then_inc(exped, 1)

            def copy(u):
                act.wait_ge(turned, u + 1)
                if u >= 3:
                    act.wait_ge(summed, u - 2)
                if u < UP:
                    n = keys(u)
                    nc.scalar.copy(prT[:, u % 3, 0:n], t_ps[u % 2][:, 0:n]).then_inc(copied, 1)
                else:
                    nc.scalar.copy(prT[:, u % 3, 0:2 * SROWS], t_ps[u % 2][:, 0:2 * SROWS])
                    nc.scalar.copy(prT[0:NS, u % 3, 2 * SROWS:3 * SROWS],
                                   t_ps[u % 2][0:NS, 2 * SROWS:3 * SROWS]).then_inc(copied, 1)

            for t in range(U + 2):
                if t < U:
                    exp(t)
                if t >= 2:
                    copy(t - 2)
                if t == NORM_AT:
                    act.wait_ge(eps_added, 1)
                    nc.scalar.activation(lr[:], lr[:], ACT.Sqrt).then_inc(rooted, 1)
                if t == NORM_AT + 4:
                    for i in range(TILES):
                        act.wait_ge(centred, 2 * TILES + i + 1)
                        nc.scalar.activation(ysig[0:ROWS[i], i], yn[0:ROWS[i], i], ACT.Sigmoid
                                             ).then_inc(sig_ready, 1)

        @block.vector
        def _(dve):
            def row_max(u):
                i, h = units[u]
                r, n = rows(u), keys(u)
                dve.wait_ge(scored, u + 1)
                if u == 0:
                    dve.wait_ge(mask_in, 32)
                if u >= 3:
                    dve.wait_ge(exped, u - 2)
                mask = pmask[:, i, 0:n] if u < UP else smask[:, h]
                nc.vector.tensor_tensor_reduce(out=sm[0:r, u % 3, 0:n], in0=s_ps[u % 3][0:r, 0:n], in1=mask,
                                               scale=1.0, scalar=-3.0e38, op0=ALU.add, op1=ALU.max,
                                               accum_out=mx[0:r, u:u + 1]).then_inc(maxed, 1)
                dve.wait_ge(maxed, u + 1)
                nc.vector.tensor_scalar(nmx[0:r, u:u + 1], mx[0:r, u:u + 1], -SCALE, None,
                                        ALU.mult).then_inc(neg_ready, 1)

            def inverse(u):
                r, n = rows(u), keys(u)
                dve.wait_ge(exped, u + 1)
                nc.vector.reciprocal(rden[0:r, u:u + 1], den[0:r, u:u + 1]).then_inc(rden_ready, 1)
                if u >= UP:
                    dve.wait_ge(rden_ready, u + 1)
                    nc.vector.tensor_scalar(pr[0:r, u % 3, 0:n], pr[0:r, u % 3, 0:n], rden[0:r, u:u + 1], None,
                                            ALU.mult).then_inc(scaled, 1)

            def norm(u):
                i, h = units[u]
                dve.wait_ge(summed, u + 1)
                if u < UP:
                    dve.wait_ge(rden_ready, u + 1)
                    if h == 0 and i >= 2:
                        dve.wait_ge(cat_turned, 2 * (i - 1))
                    nc.vector.tensor_scalar(attn[:, i % 2, h * HD:(h + 1) * HD], o_ps[u % 2][:, 0:HD],
                                            rden[:, u:u + 1], None, ALU.mult).then_inc(normed, 1)
                else:
                    for hh in range(2):
                        a = 64 * hh
                        src = o_ps[u % 2][a:a + 64, 0:SROWS].rearrange("p (j c) -> p j c", c=8)
                        ins = nc.vector.tensor_copy(catT[a:a + 64, 0:PAIRS, SEQ + DEC_T * h:SEQ + DEC_T * (h + 1)],
                                                    src[:, :, 4 * hh:4 * hh + 4])
                    ins.then_inc(normed, 1)

            def take_cat(i, b):
                dve.wait_ge(cat_turned, 2 * i + b + 1)
                n = 4 if b == 0 else 2
                nc.vector.tensor_copy(catT[:, 4 * b:4 * b + n, cols(i)],
                                      c_ps[:, 0:n * P].rearrange("p (j t) -> p j t", t=P)).then_inc(cat_taken, 1)

            def tap(k):
                for c in range(2):
                    for part in range(2):
                        if part == 0:
                            src, acc = gp[:, c, k:k + SEQ], y[:, c, 0:SEQ]
                        else:
                            src = gs[:, c, :, k:k + DEC_T]
                            acc = y[:, c, SEQ:T].rearrange("p (b t) -> p b t", t=DEC_T)
                        w = cw[:, c, k:k + 1]
                        if k == 0:
                            nc.vector.tensor_scalar(acc, src, w, cb[:, c:c + 1], ALU.mult, ALU.add
                                                    ).then_inc(tapped, 1)
                        else:
                            dve.wait_ge(tapped, 4 * k - 3 + 2 * c + part)
                            nc.vector.scalar_tensor_tensor(out=acc, in0=src, scalar=w, in1=acc, op0=ALU.mult,
                                                           op1=ALU.add).then_inc(tapped, 1)

            def take_y(n):
                dve.wait_ge(y_turned, n + 1)
                if n < 2:
                    nc.vector.tensor_copy(yt[:, 2 * n:2 * n + 2], c_ps[:].rearrange("p (i c) -> p i c", c=CH)
                                          ).then_inc(y_taken, 1)
                else:
                    nc.vector.tensor_copy(yt[0:NS, 4], c_ps[0:NS, 0:CH]).then_inc(y_taken, 1)

            def norm_y(step):
                tiles = [(i, ROWS[i]) for i in range(TILES)]
                if step == 0:
                    nc.vector.memset(lr[:], 1.0).then_inc(stats, 1)
                    dve.wait_ge(y_taken, 3)
                    for i, r in tiles:
                        nc.vector.bn_stats(st[0:r, i], yt[0:r, i]).then_inc(stats, 1)
                    for i, r in tiles:
                        dve.wait_ge(stats, i + 2)
                        nc.vector.bn_aggr(mv[0:r, i], st[0:r, i]).then_inc(aggr, 1)
                    dve.wait_ge(aggr, TILES)
                    nc.vector.tensor_scalar(lr[:, 0:4], mv[:, 0:4, 1], LN_EPS, None, ALU.add)
                    nc.vector.tensor_scalar(lr[0:NS, 4:5], mv[0:NS, 4, 1:2], LN_EPS, None, ALU.add
                                            ).then_inc(eps_added, 1)
                if step == 1:
                    dve.wait_ge(rooted, 1)
                    nc.vector.reciprocal(lr[:], lr[:]).then_inc(lr_ready, 1)
                    dve.wait_ge(lr_ready, 1)
                    for i, r in tiles:
                        nc.vector.tensor_scalar(yn[0:r, i], yt[0:r, i], mv[0:r, i, 0:1], lr[0:r, i:i + 1],
                                                ALU.subtract, ALU.mult).then_inc(centred, 1)
                if step == 2:
                    dve.wait_ge(ln_in, 32)
                if step in (2, 3):
                    for i, r in tiles:
                        dve.wait_ge(centred, TILES * (step - 2) + i + 1)
                        other, op = (lng, ALU.mult) if step == 2 else (lnb, ALU.add)
                        nc.vector.tensor_tensor(yn[0:r, i], yn[0:r, i], other[0:r], op).then_inc(centred, 1)
                if step == 5:
                    for i, r in tiles:
                        dve.wait_ge(sig_ready, i + 1)
                        nc.vector.tensor_tensor(yn[0:r, i], yn[0:r, i], ysig[0:r, i], ALU.mult).then_inc(gated, 1)

            def take_back(n):
                dve.wait_ge(g_turned, n + 1)
                for i in range(2 * n, min(2 * n + 2, TILES)):
                    r, at = ROWS[i], (i % 2) * CH
                    ins = nc.vector.tensor_copy(catT[:, PAIRS:KT, cols(i)],
                                                c_ps[:, at:at + 2 * r].rearrange("p (c t) -> p c t", t=r))
                ins.then_inc(g_taken, 1)

            dve.wait_ge(conv_in, 32)
            for t in range(U + 4):
                if t < U:
                    row_max(t)
                if 0 <= t - 1 < U:
                    inverse(t - 1)
                if t < TAPS:
                    tap(t)
                if 0 <= t - 4 < U:
                    norm(t - 4)
                if t in CATS:
                    take_cat(CATS.index(t) // 2, CATS.index(t) % 2)
                if t in Y_TURNS:
                    take_y(Y_TURNS.index(t))
                if NORM_AT <= t < NORM_AT + 6:
                    norm_y(t - NORM_AT)
                if t in BACK:
                    take_back(BACK.index(t))


def over(nc, stack, name, name_r, shape):
    at = -(-nc.sbuf_base // 32) * 32
    return (stack.enter_context(nc.sbuf_tensor(name, shape, F32)),
            nc.alloc_sbuf_tensor_at(name_r, shape, F32R, offset=at))


def wait(eng, sem, value):
    if not (isinstance(value, int) and value <= 0):
        eng.wait_ge(sem, value)


def choose(nc, d, s):
    with ExitStack() as ctx:
        sb = lambda n, sh, dt=F32: ctx.enter_context(nc.sbuf_tensor(n, sh, dt))
        sem = lambda n: ctx.enter_context(nc.semaphore(n))
        wo, wo_in = s.wo, s.wo_in
        x1 = sb("x1", [P, TILES, D])
        xr = sb("xr", [P, 2, D])
        g2 = sb("g2", [P, KT])
        g2_row = sb("g2_row", [P, D])
        ss = sb("ss2", [P, TILES])
        rt = sb("rt2", [P, TILES])
        wq = sb("wq", [P, 4, KT, P])
        keysT = sb("keysT", [P, 2, NK])
        qh = sb("qh", [P, 4, T])
        sc = sb("sc", [P, 2, TILES, 2, NK])
        v16 = sb("v16", [P, 2, TILES, 2, TOPK])
        i16 = sb("i16", [P, 2, TILES, 2, TOPK], U32)
        cand = sb("cand", [P, 2, TILES, SUMS])
        top = sb("top", [P, 2, TILES, TOPK])
        ci = sb("ci", [P, 2, TILES, TOPK], U32)
        cab = sb("cab", [P, 2, 2, TILES, TOPK], BF16)
        bits = sb("bits", [P, 2, TILES, TOPK], U32)
        terms = sb("terms", [P, 4, TILES, TOPK])
        hit = sb("hit", [P, 2, TILES, TOPK, TOPK], BF16)
        place = sb("place", [P, TOPK, TOPK], BF16)
        iota = sb("iota", [P, TOPK])
        keyf = sb("keyf", [P, 2, 2, TILES, TOPK])
        tops = sb("tops", [P, TILES, PH, TOPK])
        ef = sb("ef", [P, 2, TILES, PH, TOPK])
        gsum = sb("gsum", [P, TILES, PH])
        shift = sb("shift", [P, TILES, PH, TOPK])
        wf = sb("wf", [P, T])
        rest = sb("rest", [P, T])
        banks = [ctx.enter_context(nc.psum_tensor(f"bank{b}", [P, 512], F32)) for b in range(8)]
        assert nc.sbuf_base <= WO_AT, nc.sbuf_base - WO_AT

        x_in, g2_in, keys_in, iota_in = sem("x1_in"), sem("g2_in"), sem("keys_in"), sem("iota_in")
        wq_in = [sem(f"wq_in{b}") for b in range(4)]
        outed, added, squared, meaned = sem("outed"), sem("added"), sem("squared"), sem("meaned")
        rooted, inverted, scaled = sem("rooted"), sem("inverted"), sem("scaled")
        x_turned, h_taken, h0_ready = sem("x_turned"), sem("h_taken"), sem("h0_ready")
        x1_stored = sem("x1_stored")
        q_done, q_taken, s_done, s_taken = sem("q_done"), sem("q_taken"), sem("s_done"), sem("s_taken")
        half_step, cand_ready, top_step = sem("half_step"), sem("cand_ready"), sem("top_step")
        split_ready, hit_ready, picked, decoded = sem("split_ready"), sem("hit_ready"), sem("picked"), sem("decoded")
        shifted, gate_exp, gate_step, gates = sem("shifted"), sem("gate_exp"), sem("gate_step"), sem("gates")
        first_half_done, tops_kept, place_step = sem("first_half_done"), sem("tops_kept"), sem("place_step")
        rows_set = sem("rows_set")
        slot_turned, slot_taken, w_step = sem("slot_turned"), sem("slot_taken"), sem("w_step")
        block = ctx.enter_context(nc.Block())
        ident, catT, h2T, e1T, e2T, w3 = s.ident, s.catT, s.h2T, s.e1T, s.e2T, s.w3
        h0, row_f, w0 = s.h0, s.row_f, s.w0
        HALVES = 10
        TOPS = 5

        @block.sync
        def _(sp):
            sp.dma_start(x1[:, 0:4], d.x[0:SEQ].rearrange("(i p) n -> p i n", p=P)).then_inc(x_in, 16)
            sp.dma_start(x1[0:NS, 4], d.x[SEQ:T]).then_inc(x_in, 16)
            sp.dma_start(g2[:], d.g2).then_inc(g2_in, 16)
            sp.dma_start(g2_row[:], spread(d.g2_row, [P, D])).then_inc(g2_in, 16)
            sp.dma_start(keysT[:], d.keysT).then_inc(keys_in, 16)
            sp.dma_start(iota[:], d.iota[:, 0:TOPK]).then_inc(iota_in, 16)

            def load(it):
                for b in range(4):
                    wait(sp, q_done, 4 * it + b - 3)
                    src = d.w_q[bass.ds(4 * it + b, 1)].rearrange("o p k n -> (o p) k n")
                    sp.dma_start(wq[:, b], src).then_inc(wq_in[b], 16)

            load(0)
            with sp.Fori(1, PH // 2) as it:
                load(it)
            sp.wait_ge(added, 2 * TILES)
            sp.dma_start(d.x1[0:SEQ].rearrange("(i p) n -> p i n", p=P), x1[:, 0:4]).then_inc(x1_stored, 16)
            sp.dma_start(d.x1[SEQ:T], x1[0:NS, 4]).then_inc(x1_stored, 16)
            sp.wait_ge(x1_stored, 32)

        @block.tensor
        def _(pe):
            def out_projection(i):
                for n in range(2):
                    b = 2 * (i % 2) + n
                    wait(pe, added, 2 * i + n - 3)
                    for k in range(KT):
                        ins = pe.matmul(banks[b][0:ROWS[i]], catT[:, k, cols(i)], wo[:, k, n * 512:(n + 1) * 512],
                                        start=(k == 0), stop=(k == KT - 1))
                    ins.then_inc(outed, 1)

            def turn(i):
                r = ROWS[i]
                pe.wait_ge(scaled, i + 1)
                for n in range(2):
                    b = 4 + 2 * (i % 2) + n
                    wait(pe, h_taken, 2 * i + n - 3)
                    for j in range(4):
                        k = 4 * n + j
                        ins = pe.transpose(banks[b][:, j * r:(j + 1) * r], xr[0:r, i % 2, k * P:(k + 1) * P],
                                           ident[0:r, 0:r])
                    ins.then_inc(x_turned, 1)

            pe.wait_ge(wo_in, 16)
            for i in range(TILES + 1):
                if i < TILES:
                    out_projection(i)
                if i:
                    turn(i - 1)
            pe.wait_ge(h_taken, 2 * TILES)
            pe.wait_ge(keys_in, 16)

            def head(it, hh):
                for half in range(2):
                    b = 2 * hh + half
                    pe.wait_ge(wq_in[b], 16 * (it + 1))
                    for z in range(2):
                        q = 4 * it + b
                        wait(pe, q_taken, 2 * q + z - 3)
                        for k in range(KT):
                            ins = pe.matmul(banks[2 * half + z][:, 0:HT], wq[:, b, k], h2T[:, k, z * HT:(z + 1) * HT],
                                            start=(k == 0), stop=(k == KT - 1))
                        if z == 1:
                            ins.then_inc(q_done, 1)
                        else:
                            ins.then_inc(first_half_done, 1)
                pe.wait_ge(q_taken, 4 * (2 * it + hh + 1))
                for i in range(TILES):
                    u = 5 * (2 * it + hh) + i
                    wait(pe, s_taken, u - 3)
                    for half in range(2):
                        ins = pe.matmul(banks[4 + (5 * hh + i) % 4][0:ROWS[i], half * NK:(half + 1) * NK],
                                        qh[:, 2 * hh + half, cols(i)], keysT[:, half], start=True, stop=True)
                    ins.then_inc(s_done, 1)

            for hh in range(2):
                head(0, hh)
            with pe.Fori(1, PH // 2) as it:
                for hh in range(2):
                    head(it, hh)
            pe.wait_ge(gates, 2)
            pe.wait_ge(decoded, 4 * PH)
            pe.wait_ge(s_taken, TILES * PH)
            for n in range(3):
                for i in range(TILES):
                    r = ROWS[i]
                    src = ef[0:r, n, i] if n < 2 else tops[0:r, i]
                    dst = banks[n][:, i * P:(i + 1) * P] if i < 4 else banks[3][:, n * NS:(n + 1) * NS]
                    ins = pe.transpose(dst, src.rearrange("p h k -> p (h k)"), ident[0:r, 0:r])
            ins.then_inc(slot_turned, 1)

        @block.scalar
        def _(act):
            for i in range(TILES):
                r = ROWS[i]
                act.wait_ge(added, 2 * (i + 1))
                if i >= 2:
                    act.wait_ge(x_turned, 2 * (i - 1))
                if i == 2:
                    act.wait_ge(h0_ready, 1)
                nc.scalar.activation(xr[0:r, i % 2], x1[0:r, i], ACT.Square, accum_out=ss[0:r, i:i + 1]
                                     ).then_inc(squared, 1)
                act.wait_ge(meaned, i + 1)
                nc.scalar.activation(rt[0:r, i:i + 1], ss[0:r, i:i + 1], ACT.Sqrt).then_inc(rooted, 1)
                act.wait_ge(inverted, i + 1)
                nc.scalar.activation(xr[0:r, i % 2], x1[0:r, i], ACT.Copy, scale=rt[0:r, i:i + 1]).then_inc(scaled, 1)

            def head(it, hh):
                for half in range(2):
                    b = 2 * hh + half
                    for z in range(2):
                        q = 4 * it + b
                        act.wait_ge(q_done if z else first_half_done, q + 1)
                        if not (isinstance(it, int) and it == 0):
                            act.wait_ge(s_done, TILES * (2 * it + hh - 1))
                        nc.scalar.copy(qh[:, b, z * HT:(z + 1) * HT], banks[2 * half + z][:, 0:HT]).then_inc(q_taken, 1)
                for i in range(TILES):
                    r = ROWS[i]
                    act.wait_ge(s_done, TILES * (2 * it + hh) + i + 1)
                    if not (isinstance(it, int) and it == 0):
                        act.wait_ge(half_step, HALVES * (TILES * (2 * it + hh - 2) + i + 1))
                    nc.scalar.copy(sc[0:r, hh, i].rearrange("p a n -> p (a n)"),
                                   banks[4 + (5 * hh + i) % 4][0:r, 0:2 * NK]).then_inc(s_taken, 1)

            for hh in range(2):
                head(0, hh)
            with act.Fori(1, PH // 2) as it:
                for hh in range(2):
                    head(it, hh)
            act.wait_ge(shifted, 2)
            nc.scalar.activation(tops[:, 0:4], tops[:, 0:4], ACT.Exp)
            nc.scalar.activation(tops[0:NS, 4], tops[0:NS, 4], ACT.Exp).then_inc(gate_exp, 1)

        @block.gpsimd
        def _(pool):
            def sums(it, hh, i):
                r = ROWS[i]
                u = TILES * (2 * it + hh) + i
                pool.wait_ge(half_step, HALVES * (u + 1))
                if not (isinstance(it, int) and it == 0):
                    pool.wait_ge(top_step, TOPS * (u - 2 * TILES + 1))
                out = cand[0:r, hh, i]
                for lo, hi, a0, b1 in ((0, TOPK, 0, TOPK), (TOPK, TAIL, 1, HT8), (TAIL, SUMS, HT8, 1)):
                    na = (hi - lo) // b1
                    a = v16[0:r, hh, i, 0, a0:a0 + na].rearrange("p (a o) -> p a o", o=1)
                    b = v16[0:r, hh, i, 1, 0:b1].rearrange("p (o b) -> p o b", o=1)
                    ins = nc.gpsimd.tensor_tensor(out[:, lo:hi].rearrange("p (a b) -> p a b", b=b1),
                                                  spread(a, [r, na, b1]), spread(b, [r, na, b1]), ALU.add)
                ins.then_inc(cand_ready, 1)

            def pick(it, hh):
                n = 2 * it + hh
                for half in range(2):
                    for part, (lo, hi, r) in enumerate(((0, 4, P), (4, 5, NS))):
                        pool.wait_ge(hit_ready, 4 * n + 2 * half + part + 1)
                        for i in range(lo, hi):
                            key = keyf[0:r, hh, half, i].rearrange("p (k o) -> p k o", o=1)
                            ins = nc.gpsimd.tensor_tensor(hit[0:r, half, i], hit[0:r, half, i],
                                                          spread(key, [r, TOPK, TOPK]), ALU.mult)
                        ins.then_inc(picked, 1)

            def head(it, hh):
                for i in range(TILES):
                    sums(it, hh, i)
                if hh == 0:
                    if not (isinstance(it, int) and it == 0):
                        pick(it - 1, 1)
                else:
                    pick(it, 0)

            for hh in range(2):
                head(0, hh)
            with pool.Fori(1, PH // 2) as it:
                for hh in range(2):
                    head(it, hh)
            pick(PH // 2 - 1, 1)

        @block.vector
        def _(dve):
            dve.wait_ge(x_in, 32)
            dve.wait_ge(g2_in, 32)
            dve.wait_ge(iota_in, 16)
            nc.vector.memset(i16[:, :, 4], 0)
            nc.vector.memset(ci[:, :, 4], 0)
            nc.vector.memset(top[:, :, 4], 0.0)
            nc.vector.tensor_copy(place[:], spread(iota[:].rearrange("p (k o) -> p k o", o=1), [P, TOPK, TOPK])
                                  ).then_inc(rows_set, 1)

            def take(i):
                r = ROWS[i]
                for n in range(2):
                    dve.wait_ge(x_turned, 2 * i + n + 1)
                    g = g2[:, 4 * n:4 * n + 4].rearrange("p (k o) -> p k o", o=1)
                    nc.vector.tensor_tensor(h2T[:, 4 * n:4 * n + 4, cols(i)],
                                            banks[4 + 2 * (i % 2) + n][:, 0:4 * r].rearrange("p (k t) -> p k t", t=r),
                                            spread(g, [P, 4, r]), ALU.mult).then_inc(h_taken, 1)
                if i == 0:
                    nc.vector.tensor_tensor(h0[:], xr[:, 0], g2_row[:], ALU.mult).then_inc(h0_ready, 1)

            for i in range(TILES):
                r = ROWS[i]
                for n in range(2):
                    dve.wait_ge(outed, 2 * i + n + 1)
                    nc.vector.tensor_tensor(x1[0:r, i, n * 512:(n + 1) * 512], x1[0:r, i, n * 512:(n + 1) * 512],
                                            banks[2 * (i % 2) + n][0:r], ALU.add).then_inc(added, 1)
                dve.wait_ge(squared, i + 1)
                nc.vector.tensor_scalar(ss[0:r, i:i + 1], ss[0:r, i:i + 1], 1.0 / D, RMS_EPS, ALU.mult, ALU.add
                                        ).then_inc(meaned, 1)
                dve.wait_ge(rooted, i + 1)
                nc.vector.reciprocal(rt[0:r, i:i + 1], rt[0:r, i:i + 1]).then_inc(inverted, 1)
                if i:
                    take(i - 1)
            take(TILES - 1)

            def search(it, hh, i):
                r = ROWS[i]
                u = TILES * (2 * it + hh) + i
                dve.wait_ge(s_taken, u + 1)
                if not (isinstance(it, int) and it == 0):
                    dve.wait_ge(cand_ready, u - 2 * TILES + 1)
                x = [sc[0:r, hh, i, half] for half in range(2)]
                val = [v16[0:r, hh, i, half] for half in range(2)]
                key = [i16[0:r, hh, i, half] for half in range(2)]
                base = HALVES * u
                for half in range(2):
                    nc.vector.max(val[half][:, 0:8], x[half]).then_inc(half_step, 1)
                for half in range(2):
                    dve.wait_ge(half_step, base + 1 + half)
                    nc.vector.max_index(key[half][:, 0:8], val[half][:, 0:8], x[half]).then_inc(half_step, 1)
                for half in range(2):
                    dve.wait_ge(half_step, base + 3 + half)
                    nc.vector.match_replace(x[half], val[half][:, 0:8], x[half], -3.0e38).then_inc(half_step, 1)
                for half in range(2):
                    dve.wait_ge(half_step, base + 5 + half)
                    nc.vector.max(val[half][:, 8:16], x[half]).then_inc(half_step, 1)
                for half in range(2):
                    dve.wait_ge(half_step, base + 7 + half)
                    nc.vector.max_index(key[half][:, 8:16], val[half][:, 8:16], x[half]).then_inc(half_step, 1)

            def search_sums(it, hh, i):
                r = ROWS[i]
                u = TILES * (2 * it + hh) + i
                dve.wait_ge(cand_ready, u + 1)
                x, val, at = cand[0:r, hh, i], top[0:r, hh, i], ci[0:r, hh, i]
                base = TOPS * u
                nc.vector.max(val[:, 0:8], x).then_inc(top_step, 1)
                dve.wait_ge(top_step, base + 1)
                nc.vector.max_index(at[:, 0:8], val[:, 0:8], x).then_inc(top_step, 1)
                dve.wait_ge(top_step, base + 2)
                nc.vector.match_replace(x, val[:, 0:8], x, -3.0e38).then_inc(top_step, 1)
                dve.wait_ge(top_step, base + 3)
                nc.vector.max(val[:, 8:16], x).then_inc(top_step, 1)
                dve.wait_ge(top_step, base + 4)
                nc.vector.max_index(at[:, 8:16], val[:, 8:16], x).then_inc(top_step, 1)

            def split(it, hh):
                n = 2 * it + hh
                dve.wait_ge(top_step, TOPS * TILES * (n + 1))
                dve.wait_ge(half_step, HALVES * TILES * (n + 1))
                if not (isinstance(it, int) and it == 0):
                    dve.wait_ge(picked, 4 * (n - 1))
                for half in range(2):
                    nc.vector.tensor_copy(keyf[:, hh, half], i16[:, hh, :, half])
                p, row, column = ci[:, hh], bits[:, 0], bits[:, 1]
                wait(dve, place_step, 6 * n)
                nc.vector.tensor_scalar(row, p, 3, None, ALU.logical_shift_right).then_inc(place_step, 1)
                nc.vector.tensor_scalar(column, p, 7, None, ALU.bitwise_and).then_inc(place_step, 1)
                dve.wait_ge(place_step, 6 * n + 2)
                wait(dve, split_ready, 2 * n)
                nc.vector.tensor_scalar(terms[:, 0], row, 1.0, 0.0, ALU.subtract, ALU.max).then_inc(place_step, 1)
                nc.vector.scalar_tensor_tensor(out=terms[:, 1], in0=p, scalar=float(TAIL), in1=column,
                                               op0=ALU.is_ge, op1=ALU.mult).then_inc(place_step, 1)
                nc.vector.scalar_tensor_tensor(out=terms[:, 2], in0=p, scalar=float(TAIL), in1=column,
                                               op0=ALU.is_lt, op1=ALU.mult).then_inc(place_step, 1)
                nc.vector.tensor_scalar(terms[:, 3], row, 1.0, 8.0, ALU.is_equal, ALU.mult).then_inc(place_step, 1)
                dve.wait_ge(place_step, 6 * n + 6)
                for half in range(2):
                    nc.vector.tensor_tensor(cab[:, hh, half], terms[:, 2 * half], terms[:, 2 * half + 1], ALU.add
                                            ).then_inc(split_ready, 1)
                dst = tops[:, :, bass.ds(n, 1)].rearrange("p i o k -> p i (o k)")
                nc.vector.tensor_copy(dst, top[:, hh]).then_inc(tops_kept, 1)

            def hits(it, hh):
                n = 2 * it + hh
                for half in range(2):
                    dve.wait_ge(split_ready, 2 * (n + 1))
                    wait(dve, decoded, 2 * (2 * n + half - 1))
                    for lo, hi, r in ((0, 4, P), (4, 5, NS)):
                        for i in range(lo, hi):
                            slot = cab[0:r, hh, half, i].rearrange("p (o j) -> p o j", o=1)
                            ins = nc.vector.tensor_tensor(hit[0:r, half, i], spread(slot, [r, TOPK, TOPK]),
                                                          place[0:r], ALU.is_equal)
                        ins.then_inc(hit_ready, 1)

            def decode(it, hh):
                n = 2 * it + hh
                for half in range(2):
                    for g, (lo, hi, r) in enumerate(((0, 4, P), (4, 5, NS))):
                        dve.wait_ge(picked, 4 * n + 2 * half + g + 1)
                        dst = ef[0:r, half, lo:hi, bass.ds(n, 1)].rearrange("p i o k -> p i (o k)")
                        nc.vector.tensor_reduce(dst, hit[0:r, half, lo:hi].rearrange("p i k j -> p i j k"), AX_X,
                                                ALU.add).then_inc(decoded, 1)

            def head(it, hh):
                first = isinstance(it, int) and it == 0
                for i in range(TILES):
                    search(it, hh, i)
                    if i:
                        search_sums(it, hh, i - 1)
                search_sums(it, hh, TILES - 1)
                split(it, hh)
                if hh == 1:
                    decode(it, 0)
                elif not first:
                    decode(it - 1, 1)
                hits(it, hh)

            dve.wait_ge(rows_set, 1)
            for hh in range(2):
                head(0, hh)
            for it in range(1, PH // 2):
                for hh in range(2):
                    head(it, hh)
            decode(PH // 2 - 1, 1)
            dve.wait_ge(tops_kept, PH)
            parts = ((0, 4, P), (4, 5, NS))
            for lo, hi, r in parts:
                for i in range(lo, hi):
                    ins = nc.vector.tensor_tensor(shift[0:r, i], tops[0:r, i], spread(tops[0:r, i, :, 0:1], [r, PH, TOPK]),
                                                  ALU.subtract)
                ins.then_inc(gate_step, 1)
            for n, (lo, hi, r) in enumerate(parts):
                dve.wait_ge(gate_step, n + 1)
                nc.vector.tensor_copy(tops[0:r, lo:hi], shift[0:r, lo:hi]).then_inc(shifted, 1)
            dve.wait_ge(gate_exp, 1)
            for lo, hi, r in parts:
                nc.vector.tensor_reduce(gsum[0:r, lo:hi], tops[0:r, lo:hi], AX_X, ALU.add).then_inc(gate_step, 1)
            for n, (lo, hi, r) in enumerate(parts):
                dve.wait_ge(gate_step, 2 + n + 1)
                nc.vector.reciprocal(gsum[0:r, lo:hi], gsum[0:r, lo:hi]).then_inc(gate_step, 1)
            for n, (lo, hi, r) in enumerate(parts):
                dve.wait_ge(gate_step, 4 + n + 1)
                for i in range(lo, hi):
                    inv = gsum[0:r, i].rearrange("p (h o) -> p h o", o=1)
                    ins = nc.vector.tensor_tensor(tops[0:r, i], tops[0:r, i], spread(inv, [r, PH, TOPK]), ALU.mult)
                ins.then_inc(gates, 1)
            dve.wait_ge(decoded, 4 * PH)
            flat = lambda x: x.rearrange("p h k -> p (h k)")
            nc.vector.scalar_tensor_tensor(out=row_f[:], in0=flat(ef[:, 0, 0]), scalar=float(NK),
                                           in1=flat(ef[:, 1, 0]), op0=ALU.mult, op1=ALU.add)
            dve.wait_ge(gates, 1)
            nc.vector.tensor_copy(w0[:], flat(tops[:, 0]))
            dve.wait_ge(slot_turned, 1)
            for n, dst in enumerate((e1T, e2T, wf)):
                nc.vector.tensor_copy(dst[:, 0:SEQ], banks[n][:])
                nc.vector.tensor_copy(dst[:, SEQ:T], banks[3][:, n * NS:(n + 1) * NS]).then_inc(slot_taken, 1)
            dve.wait_ge(slot_taken, 3)
            nc.vector.tensor_copy(w3[:, 0], wf[:]).then_inc(w_step, 1)
            dve.wait_ge(w_step, 1)
            nc.vector.tensor_tensor(rest[:], wf[:], w3[:, 0], ALU.subtract).then_inc(w_step, 1)
            dve.wait_ge(w_step, 2)
            nc.vector.tensor_copy(w3[:, 1], rest[:]).then_inc(w_step, 1)
            dve.wait_ge(w_step, 3)
            nc.vector.tensor_tensor(w3[:, 2], rest[:], w3[:, 1], ALU.subtract).then_inc(w_step, 1)


def experts(nc, d, s):
    with ExitStack() as ctx:
        sb = lambda n, sh, dt=F32: ctx.enter_context(nc.sbuf_tensor(n, sh, dt))
        sem = lambda n: ctx.enter_context(nc.semaphore(n))
        gate, p_high = over(nc, ctx, "gate", "p_high", [P, 2, CPP, DT])
        p_low = sb("p_low", [P, 2 * CG, DT], F32R)
        u, u_low = over(nc, ctx, "u", "u_low", [P, 2, KT, P])
        u_high = sb("u_high", [P, 2, KT, P], F32R)
        vv, v_low = over(nc, ctx, "vv", "v_low", [P, 2, CG, VC])
        v_high = sb("v_high", [P, 2, CG, VC], F32R)
        h_high = sb("h_high", [P, KT, DT], F32R)
        gel = sb("gel", [P, 4, DT])
        rows = sb("rows", [P, ROW_BUFS, D])
        row_u = sb("row_u", [P, FPP], U32)
        dots = sb("dots", [P, FPP])
        coef = sb("coef", [P, SLOTS])
        coef_p = sb("coef_p", [P, FPP])
        hot = sb("hot", [P, HOTS, NK, TB], BF16)
        eq2 = sb("eq2", [P, CPP, UT_MAX], BF16)
        wsec = sb("wsec", [P, 2, 3, CPP, UT_MAX], BF16)
        iota_f = sb("iota_f", [P, NK])
        count_k = sb("count_k", [P, NK, TB], BF16)
        count_c = sb("count_c", [P, CPP, UT_MAX], BF16)
        a_ps = [ctx.enter_context(nc.psum_tensor(f"a_ps{b}", [P, 512], F32)) for b in range(2)]
        y_ps = [ctx.enter_context(nc.psum_tensor(f"y_ps{b}", [P, 512], F32)) for b in range(4)]
        g_ps = [ctx.enter_context(nc.psum_tensor(f"g_ps{b}", [P, 512], F32)) for b in range(2)]

        u_in = [sem(f"u_in{b}") for b in range(2)]
        v_in = [sem(f"v_in{b}") for b in range(2)]
        iota_in, consts = sem("iota_in"), sem("consts")
        a_done, acted, gated = sem("a_done"), sem("acted"), sem("gated")
        v_done, y_added = sem("v_done"), sem("y_added")
        eq_ready, w_ready = sem("eq_ready"), sem("w_ready")
        hot_ready, moved = sem("hot_ready"), sem("moved")
        g_done, built = sem("g_done"), sem("built")
        h_rounded, h_split = sem("h_rounded"), sem("h_split")
        u_rounded, u_split = sem("u_rounded"), sem("u_split")
        v_rounded, v_split = sem("v_rounded"), sem("v_split")
        p_rounded, p_split = sem("p_rounded"), sem("p_split")
        fetched = [sem(f"fetched{n}") for n in range(ROW_BUFS)]
        numbered, row_used, y0_zero = sem("numbered"), sem("row_used"), sem("y0_zero")
        buffer_free = sem("buffer_free")
        dots_gelu, coef_ready = sem("dots_gelu"), sem("coef_ready")
        block = ctx.enter_context(nc.Block())
        h0, row_f, w0, y0 = s.h0, s.row_f, s.w0, s.y0
        h2T, h_low, e1T, e2T, w3, yT = s.h2T, s.h_low, s.e1T, s.e2T, s.w3, s.yT
        unit_of = [w for w, m in enumerate(m for g in UNITS for m in g) for _ in range(m)]
        unit_at = [unit_of.index(w) for w in range(UPP)]

        def slab(tensor, par, c):
            return tensor[:, bass.ds(par, 1), c].rearrange("p o t -> p (o t)")

        def run_parts(eng, group):
            for gg in range(GROUPS):
                group(0, gg, True, 0)
            with eng.Fori(1, PPH) as part:
                for gg in range(GROUPS):
                    group(part, gg, True, 0)
            with eng.Fori(PPH, PARTS - 1) as part:
                for gg in range(GROUPS):
                    group(part, gg, True, 1)
            for gg in range(GROUPS):
                group(PARTS - 1, gg, False, 1)

        def steps(part, gg, build, phase):
            out = group_steps(gg, build, not (isinstance(part, int) and part == 0 and gg == 0),
                              isinstance(part, int) and part == PARTS - 1 and gg == GROUPS - 1, phase)
            if isinstance(part, int) and part == 0 and gg == 1:
                out.remove(("p", -1))
            return out

        def chunk(part, gg, c):
            q = CG * (GROUPS * part + gg) + c
            if c < 0:
                part, gg = before(part, gg)
            if c == CG:
                part, gg = (part, gg + 1) if gg < GROUPS - 1 else (part + 1, 0)
            return part, gg, c % CG, q

        def before(part, gg):
            return (part, gg - 1) if gg else (part - 1, GROUPS - 1)

        @block.sync
        def _(sp):
            sp.dma_start(iota_f[:], d.iota).then_inc(iota_in, 16)

            def load_u(part, gg, c):
                part, gg, c, q = chunk(part, gg, c)
                wait(sp, a_done, q - 1)
                sp.dma_start(u[:, c % 2], d.uT[bass.ds(q, 1)].rearrange("o p k e -> (o p) k e")
                             ).then_inc(u_in[c % 2], 16)

            def load_v(part, gg, m):
                g = GROUPS * part + gg
                wait(sp, v_done, KT // VS * (VS * g + m - 1))
                sp.dma_start(vv[:, m % 2], d.v[:, bass.ds(g, 1), :, m * VC:(m + 1) * VC
                                               ].rearrange("p o c n -> p (o c) n")).then_inc(v_in[m % 2], 16)

            def group(part, gg, build, phase):
                for what, *at in steps(part, gg, False, phase):
                    if what == "u":
                        load_u(part, gg, *at)
                    if what == "w":
                        load_v(*before(part, gg), *at) if at[0] < VS else load_v(part, gg, 0)

            load_u(0, 0, 0)
            run_parts(sp, group)
            for m in range(1, VS):
                load_v(PARTS - 1, GROUPS - 1, m)

        @block.tensor
        def _(pe):
            def activate(part, gg, c, tiles=range(KT)):
                q = CG * (GROUPS * part + gg) + c
                if tiles[0] == 0:
                    pe.wait_ge(u_split, q + 1)
                    wait(pe, acted, q - 1)
                for k in tiles:
                    high, low = h_high[:, k], h_low[:, k, P:T]
                    for n, (x, y) in enumerate(((u_high, high), (u_high, low), (u_low, high))):
                        ins = pe.matmul(a_ps[c % 2][:, 0:DT], x[:, c % 2, k], y,
                                        start=(k == 0 and n == 0), stop=(k == KT - 1 and n == 2))
                if tiles[-1] == KT - 1:
                    ins.then_inc(a_done, 1)

            def weigh(part, gg, m):
                g = GROUPS * part + gg
                q = KT * g + m
                of, at = m * P // VC, m * P % VC
                if at == 0:
                    pe.wait_ge(v_split, VS * g + of + 1)
                if m == 0:
                    pe.wait_ge(p_split, CG * (g + 1))
                wait(pe, y_added, q - 3)
                for c in range(CG):
                    high = slab(p_high, part % 2, CG * gg + c)
                    low = p_low[:, CG * (gg % 2) + c]
                    for n, (x, y) in enumerate(((v_high, high), (v_high, low), (v_low, high))):
                        ins = pe.matmul(y_ps[m % 4][:, 0:DT], x[:, of % 2, c, at:at + P], y,
                                        start=(c == 0 and n == 0), stop=(c == CG - 1 and n == 2))
                ins.then_inc(v_done, 1)

            def gates(part, n):
                m, w = BPP * part + n, unit_of[n]
                if unit_at[w] == n:
                    pe.wait_ge(w_ready, UPP * part + w + 1)
                pe.wait_ge(hot_ready, m + 1)
                wait(pe, built, m - 1)
                for t in range(TB):
                    out = g_ps[n % 2][:, t * 3 * CPP:(t + 1) * 3 * CPP].rearrange("p (w c) -> p w c", w=3)
                    ins = pe.matmul(out, hot[:, n % HOTS, :, t], wsec[:, w % 2, :, :, (n - unit_at[w]) * TB + t],
                                    start=True, stop=True)
                ins.then_inc(g_done, 1)

            for what, n in build_steps():
                if what == "b":
                    gates(0, n)
                    if n == FIRST_A[0]:
                        pe.wait_ge(h_split, KT)
                    if n in FIRST_A:
                        c, k = divmod(FIRST_K * FIRST_A.index(n), KT)
                        activate(0, 0, c, range(k, k + FIRST_K))

            def group(part, gg, build, phase):
                for what, *at in steps(part, gg, build, phase):
                    if what == "a" and not (isinstance(part, int) and part == gg == 0):
                        activate(part, gg, *at)
                    if what == "v":
                        weigh(*before(part, gg), *at)
                    if what == "b":
                        gates(part + 1, *at)

            run_parts(pe, group)
            for m in range(KT):
                weigh(PARTS - 1, GROUPS - 1, m)

        @block.scalar
        def _(act):
            def round_u(part, gg, c):
                part, gg, c, q = chunk(part, gg, c)
                act.wait_ge(u_in[c % 2], 16 * (2 * (GROUPS * part + gg) + c // 2 + 1))
                nc.scalar.copy(u_high[:, c % 2], u[:, c % 2]).then_inc(u_rounded, 1)

            def round_v(part, gg, m):
                act.wait_ge(v_in[m % 2], 16 * (VS // 2 * (GROUPS * part + gg) + m // 2 + 1))
                nc.scalar.copy(v_high[:, m % 2], vv[:, m % 2]).then_inc(v_rounded, 1)

            def gelu(part, gg, c):
                q = CG * (GROUPS * part + gg) + c
                wait(act, p_split, q - 3)
                act.wait_ge(a_done, q + 1)
                nc.scalar.activation(gel[:, c % 4], a_ps[c % 2][:, 0:DT], ACT.Gelu_apprx_tanh).then_inc(acted, 1)

            def round_p(part, gg, c):
                part, gg, c, q = chunk(part, gg, c)
                act.wait_ge(gated, q + 1)
                nc.scalar.copy(slab(p_high, part % 2, CG * gg + c), gel[:, c % 4]).then_inc(p_rounded, 1)

            def group(part, gg, build, phase):
                for what, *at in steps(part, gg, False, phase):
                    if what == "u":
                        round_u(part, gg, *at)
                    if what == "a":
                        gelu(part, gg, *at)
                    if what == "p":
                        round_p(part, gg, *at)
                    if what == "w":
                        round_v(*before(part, gg), *at) if at[0] < VS else round_v(part, gg, 0)
                    if what == "c":
                        act.wait_ge(row_used, FPP * (part + 1))
                        nc.scalar.activation(dots[:], dots[:], ACT.Gelu_apprx_tanh).then_inc(dots_gelu, 1)

            for k in range(KT):
                nc.scalar.copy(h_high[:, k], h2T[:, k, P:T]).then_inc(h_rounded, 1)
            round_u(0, 0, 0)
            run_parts(act, group)
            round_p(PARTS - 1, GROUPS - 1, CG - 1)
            for m in range(1, VS):
                round_v(PARTS - 1, GROUPS - 1, m)

        @block.gpsimd
        def _(pool):
            def low(part, whole, high, rounded, value):
                pool.wait_ge(rounded, value)
                return nc.gpsimd.tensor_tensor(part, whole, high.bitcast(F32), ALU.subtract)

            def split_u(part, gg, c):
                part, gg, c, q = chunk(part, gg, c)
                low(u_low[:, c % 2], u[:, c % 2], u_high[:, c % 2], u_rounded, q + 1).then_inc(u_split, 1)

            def split_v(part, gg, m):
                low(v_low[:, m % 2], vv[:, m % 2], v_high[:, m % 2], v_rounded,
                    VS * (GROUPS * part + gg) + m + 1).then_inc(v_split, 1)

            def split_p(part, gg, c):
                part, gg, c, q = chunk(part, gg, c)
                wait(pool, v_done, KT * (GROUPS * part + gg - 1))
                low(p_low[:, CG * (gg % 2) + c], gel[:, c % 4],
                    slab(p_high, part % 2, CG * gg + c), p_rounded, q + 1).then_inc(p_split, 1)

            def fetch(part, j, phase):
                if j == 0:
                    pool.wait_ge(numbered, part + 1)
                wait(pool, row_used, FPP * part + j - ROW_BUFS + 1)
                pool.sem_inc(buffer_free, 1)
                table = d.v.rearrange("a g c n -> (a g c) n") if phase else d.u_rows
                nc.gpsimd.indirect_dma_start(rows[:, j % ROW_BUFS], None, table,
                                             bass.IndirectOffsetOnAxis(ap=row_u[:, j:j + 1], axis=0)
                                             ).then_inc(fetched[j % ROW_BUFS], 16)

            def group(part, gg, build, phase):
                for what, *at in steps(part, gg, False, phase):
                    if what == "i":
                        for j in range(ROW_BUFS - 1):
                            fetch(part, j, phase)
                    if what == "d" and at[0] + ROW_BUFS - 1 < FPP:
                        fetch(part, at[0] + ROW_BUFS - 1, phase)
                    if what == "u":
                        split_u(part, gg, *at)
                    if what == "p":
                        split_p(part, gg, *at)
                    if what == "w":
                        split_v(*before(part, gg), *at) if at[0] < VS else split_v(part, gg, 0)

            for k in range(KT):
                low(h_low[:, k, P:T], h2T[:, k, P:T], h_high[:, k], h_rounded, k + 1).then_inc(h_split, 1)
            split_u(0, 0, 0)
            run_parts(pool, group)
            split_p(PARTS - 1, GROUPS - 1, CG - 1)
            for m in range(1, VS):
                split_v(PARTS - 1, GROUPS - 1, m)

        @block.vector
        def _(dve):
            dve.wait_ge(iota_in, 16)
            nc.vector.memset(yT[:, :, P:T], 0.0)
            nc.vector.memset(y0[:], 0.0).then_inc(y0_zero, 1)
            iota = iota_f[:].rearrange("p (k o) -> p k o", o=1)
            nc.vector.tensor_copy(count_c[:], spread(iota[:, 0:CPP], [P, CPP, UT_MAX]))
            nc.vector.tensor_copy(count_k[:], spread(iota, [P, NK, TB])).then_inc(consts, 1)

            def one_hots(part, n):
                wait(dve, g_done, BPP * part + n - (HOTS - 1))
                dve.wait_ge(consts, 1)
                key = e1T[:, P + n * TB:P + (n + 1) * TB].rearrange("p (o t) -> p o t", o=1)
                nc.vector.tensor_tensor(hot[:, n % HOTS], count_k[:], spread(key, [P, NK, TB]), ALU.is_equal
                                        ).then_inc(hot_ready, 1)

            def second(part, w):
                uw = UPP * part + w
                t0 = unit_at[w] * TB
                n = unit_of.count(w) * TB
                key = e2T[:, P + t0:P + t0 + n].rearrange("p (o t) -> p o t", o=1)
                if w == 0:
                    wait(dve, moved, part)
                wait(dve, w_ready, uw)
                dve.wait_ge(consts, 1)
                nc.vector.tensor_tensor(eq2[:, :, 0:n], count_c[:, :, 0:n], spread(key, [P, CPP, n]), ALU.is_equal
                                        ).then_inc(eq_ready, 1)
                wait(dve, g_done, BPP * part + (unit_at[w - 1] if w else unit_at[UPP - 1] - BPP))
                dve.wait_ge(eq_ready, uw + 1)
                for i in range(3):
                    wi = w3[:, i, P + t0:P + t0 + n].rearrange("p (o t) -> p o t", o=1)
                    ins = nc.vector.tensor_tensor(wsec[:, w % 2, i, :, 0:n], eq2[:, :, 0:n], spread(wi, [P, CPP, n]),
                                                  ALU.mult)
                ins.then_inc(w_ready, 1)
                if w == UPP - 1:
                    nc.vector.tensor_scalar(e2T[:], e2T[:], -float(CPP), None, ALU.add).then_inc(moved, 1)

            def take_gates(part, n):
                dve.wait_ge(g_done, BPP * part + n + 1)
                if n == 0:
                    wait(dve, v_done, KT * GROUPS * (part - 1))
                dve.wait_ge(consts, 1)
                src = g_ps[n % 2][:, 0:TB * 3 * CPP].rearrange("p (t w c) -> p t c w", t=TB, w=3)
                dst = gate[:, bass.ds(part % 2, 1), :, n * TB:(n + 1) * TB].rearrange("p o c t -> p t (o c)")
                nc.vector.tensor_reduce(dst, src, AX_X, ALU.add).then_inc(built, 1)

            def multiply(part, gg, c):
                q = CG * (GROUPS * part + gg) + c
                if gg == 0 and c == 0:
                    dve.wait_ge(built, BPP * (part + 1))
                dve.wait_ge(acted, q + 1)
                x = gel[:, c % 4]
                nc.vector.tensor_tensor(x, x, slab(gate, part % 2, CG * gg + c), ALU.mult).then_inc(gated, 1)

            def add(part, gg, m):
                q = KT * (GROUPS * part + gg) + m
                wait(dve, y_added, q - KT + 1)
                dve.wait_ge(v_done, q + 1)
                acc = yT[:, m, P:T]
                nc.vector.tensor_tensor(acc, acc, y_ps[m % 4][:, 0:DT], ALU.add).then_inc(y_added, 1)

            def number(part, phase):
                own = bass.ds(FPP * (part - PPH * phase), FPP)
                wait(dve, row_used, FPP * part)
                dve.wait_ge(consts, 1)
                ins = nc.vector.tensor_scalar(row_u[:], row_f[:, own], 1.0, None, ALU.mult)
                if phase:
                    dve.wait_ge(coef_ready, PPH)
                    ins = nc.vector.tensor_scalar(coef_p[:], coef[:, own], 1.0, None, ALU.mult)
                ins.then_inc(numbered, 1)

            def use_row(part, j, phase):
                row = rows[:, j % ROW_BUFS]
                dve.wait_ge(fetched[j % ROW_BUFS], 16 * (FPP // ROW_BUFS * part + j // ROW_BUFS + 1))
                if phase:
                    dve.wait_ge(row_used, FPP * part + j - 1)
                    if j == 0:
                        dve.wait_ge(numbered, part + 1)
                    dve.wait_ge(y0_zero, 1)
                    nc.vector.scalar_tensor_tensor(out=y0[:, j % 2], in0=row, scalar=coef_p[:, j:j + 1],
                                                   in1=y0[:, j % 2], op0=ALU.mult, op1=ALU.add
                                                   ).then_inc(row_used, 1)
                else:
                    nc.vector.tensor_tensor_reduce(out=row, in0=row, in1=h0[:], scale=1.0, scalar=0.0,
                                                   op0=ALU.mult, op1=ALU.add, accum_out=dots[:, j:j + 1]
                                                   ).then_inc(row_used, 1)

            def coefficients(part):
                own = bass.ds(FPP * part, FPP)
                dve.wait_ge(dots_gelu, part + 1)
                nc.vector.tensor_tensor(coef[:, own], dots[:], w0[:, own], ALU.mult).then_inc(coef_ready, 1)

            def build(part, what, n):
                {"s": second, "h": one_hots, "b": take_gates}[what](part, n)

            for what, n in build_steps():
                build(0, what, n)

            def group(part, gg, do_build, phase):
                for what, *at in steps(part, gg, do_build, phase):
                    if what == "a":
                        multiply(part, gg, *at)
                    elif what == "v":
                        add(*before(part, gg), *at)
                    elif what == "i":
                        number(part, phase)
                    elif what == "d":
                        use_row(part, *at, phase)
                    elif what == "c":
                        coefficients(part)
                    elif what in "shb":
                        build(part + 1, what, *at)

            run_parts(dve, group)
            for m in range(KT):
                add(PARTS - 1, GROUPS - 1, m)


def finish(nc, d, s):
    with ExitStack() as ctx:
        sb = lambda n, sh, dt=F32: ctx.enter_context(nc.sbuf_tensor(n, sh, dt))
        sem = lambda n: ctx.enter_context(nc.semaphore(n))
        x1 = sb("x1_back", [P, TILES, D])
        xo = sb("xo", [P, TILES, D])
        gf = sb("gf", [P, D])
        ss = sb("ss3", [P, TILES])
        rt = sb("rt3", [P, TILES])
        banks = [ctx.enter_context(nc.psum_tensor(f"f_ps{b}", [P, 512], F32)) for b in range(4)]
        x_in, g_in = sem("x_in"), sem("g_in")
        turned, added, squared, meaned = sem("turned"), sem("added"), sem("squared"), sem("meaned")
        rooted, inverted, scaled, done, stored = (sem(x) for x in ("rooted", "inverted", "scaled", "done", "stored"))
        block = ctx.enter_context(nc.Block())
        ident, yT, y0 = s.ident, s.yT, s.y0

        @block.sync
        def _(sp):
            sp.dma_start(x1[:, 0:4], d.x1[0:SEQ].rearrange("(i p) n -> p i n", p=P)).then_inc(x_in, 16)
            sp.dma_start(x1[0:NS, 4], d.x1[SEQ:T]).then_inc(x_in, 16)
            sp.dma_start(gf[:], spread(d.gf, [P, D])).then_inc(g_in, 16)
            for i in range(TILES):
                sp.wait_ge(done, i + 1)
                sp.dma_start(d.out_y[i * P:i * P + ROWS[i]], xo[0:ROWS[i], i]).then_inc(stored, 16)
            sp.wait_ge(stored, 16 * TILES)

        @block.tensor
        def _(pe):
            for i in range(1, TILES):
                for n in range(2):
                    q = 2 * i + n
                    wait(pe, added, q - 3)
                    for j in range(4):
                        ins = pe.transpose(banks[q % 4][0:ROWS[i], j * P:(j + 1) * P], yT[:, 4 * n + j, cols(i)],
                                           ident[:])
                    ins.then_inc(turned, 1)

        @block.scalar
        def _(act):
            for i in range(TILES):
                r = ROWS[i]
                act.wait_ge(added, 2 * (i + 1))
                nc.scalar.activation(xo[0:r, i], x1[0:r, i], ACT.Square, accum_out=ss[0:r, i:i + 1]
                                     ).then_inc(squared, 1)
                act.wait_ge(meaned, i + 1)
                nc.scalar.activation(rt[0:r, i:i + 1], ss[0:r, i:i + 1], ACT.Sqrt).then_inc(rooted, 1)
                act.wait_ge(inverted, i + 1)
                nc.scalar.activation(xo[0:r, i], x1[0:r, i], ACT.Copy, scale=rt[0:r, i:i + 1]).then_inc(scaled, 1)

        @block.vector
        def _(dve):
            dve.wait_ge(x_in, 32)
            dve.wait_ge(g_in, 16)

            def gain(i):
                r = ROWS[i]
                dve.wait_ge(scaled, i + 1)
                nc.vector.tensor_tensor(xo[0:r, i], xo[0:r, i], gf[0:r], ALU.mult).then_inc(done, 1)

            for i in range(TILES):
                r = ROWS[i]
                for n in range(2):
                    q = 2 * i + n
                    if i == 0:
                        wait(dve, added, n)
                        nc.vector.tensor_tensor(x1[:, 0], x1[:, 0], y0[:, n], ALU.add).then_inc(added, 1)
                        continue
                    dve.wait_ge(turned, q - 1)
                    half = x1[0:r, i, n * 512:(n + 1) * 512]
                    nc.vector.tensor_tensor(half, half, banks[q % 4][0:r], ALU.add).then_inc(added, 1)
                dve.wait_ge(squared, i + 1)
                nc.vector.tensor_scalar(ss[0:r, i:i + 1], ss[0:r, i:i + 1], 1.0 / D, RMS_EPS, ALU.mult, ALU.add
                                        ).then_inc(meaned, 1)
                dve.wait_ge(rooted, i + 1)
                nc.vector.reciprocal(rt[0:r, i:i + 1], rt[0:r, i:i + 1]).then_inc(inverted, 1)
                if i:
                    gain(i - 1)
            gain(TILES - 1)


class Names(dict):

    def __getattr__(self, name):
        return self[name]


def build(nc, d):
    with ExitStack() as ctx:
        def kept(stack, name, shape, dt=F32):
            return stack.enter_context(nc.sbuf_tensor(name, shape, dt))

        s = Names()
        s["ident"] = kept(ctx, "ident", [P, P])
        s["catT"] = s["yT"] = kept(ctx, "catT_then_yT", [P, KT, T])
        with ExitStack() as first:
            s["qT"] = kept(first, "qT", [P, PAIRS, T])
            s["kT"] = kept(first, "kT", [P, PAIRS, T])
            s["v"] = kept(first, "v", [P, TILES, AW])
            s["gp"] = kept(first, "gp", [P, 2, TAPS - 1 + SEQ])
            s["gs"] = kept(first, "gs", [P, 2, DEC_B, TAPS - 1 + DEC_T])
            project(nc, d, s)
            s["wo"] = nc.alloc_sbuf_tensor_at("wo", [P, KT, D], F32, offset=WO_AT)
            s["wo_in"] = ctx.enter_context(nc.semaphore("wo_in"))
            mix(nc, d, s)
        s["h2T"], s["h_low"] = over(nc, ctx, "h2T", "h_low", [P, KT, T])
        s["e1T"] = kept(ctx, "e1T", [P, T], BF16)
        s["e2T"] = kept(ctx, "e2T", [P, T], BF16)
        s["w3"] = kept(ctx, "w3", [P, 3, T], BF16)
        s["h0"] = kept(ctx, "h0", [P, D])
        s["row_f"] = kept(ctx, "row_f", [P, SLOTS])
        s["w0"] = kept(ctx, "w0", [P, SLOTS])
        choose(nc, d, s)
        s["y0"] = kept(ctx, "y0", [P, 2, D])
        experts(nc, d, s)
        finish(nc, d, s)


def kernel(x_prompt, x_sample, cache_k, cache_v, state_conv, norm1_g, w_in, conv_w, conv_b,
           conv_ln_g, conv_ln_b, w_out, norm2_g, w_query, sub_keys1, sub_keys2,
           expert_u, expert_v, final_g):
    import concourse.bacc as bacc
    from concourse.bass_utils import run_bass_kernel_spmd

    f = lambda a: np.asarray(a)
    c = np.ascontiguousarray
    cos, sin = rope_tables()
    x = np.concatenate([f(x_prompt).reshape(SEQ, D), f(x_sample).reshape(NS, D)])
    given = {
        "x": x,
        "xT": c(x.T.reshape(KT, P, T).transpose(1, 0, 2)),
        "g1": c(f(norm1_g).reshape(KT, P).T),
        "w_in": c(f(w_in)[0].reshape(KT, P, NCB, CB).transpose(2, 1, 0, 3)),
        "cos": cos,
        "sin": sin,
        "ident": np.eye(P, dtype=np.float32),
        "state": c(f(state_conv)[0].transpose(2, 0, 1).reshape(2, P, DEC_B, TAPS - 1).transpose(1, 0, 2, 3)),
        "state_rows": c(f(state_conv)[0]),
        "ckT": c(f(cache_k)[0].reshape(DEC_B, PAST, PAIRS, P).transpose(0, 3, 2, 1)),
        "cv": c(f(cache_v)[0].reshape(DEC_B, 2, P, AW).transpose(0, 2, 1, 3)),
        "pmask": prompt_mask(),
        "smask": sample_mask(),
        "conv_w": c(f(conv_w)[0].T.reshape(2, P, TAPS).transpose(1, 0, 2)),
        "conv_b": c(f(conv_b)[0].reshape(2, P).T),
        "ln_g": c(f(conv_ln_g)[0].reshape(1, CH)),
        "ln_b": c(f(conv_ln_b)[0].reshape(1, CH)),
        "w_out": c(f(w_out)[0].reshape(KT, P, D).transpose(1, 0, 2)),
        "g2": c(f(norm2_g)[0].reshape(KT, P).T),
        "w_q": c(f(w_query)[0].reshape(KT, P, 2 * PH, P).transpose(2, 1, 0, 3)),
        "keysT": c(np.stack([f(sub_keys1)[0].T, f(sub_keys2)[0].T], 1)),
        "uT": c(f(expert_u)[0].reshape(NK, NK, KT, P).transpose(1, 3, 2, 0)),
        "v": c(f(expert_v)[0].reshape(NK, NG, CG, D)),
        "u_rows": c(f(expert_u)[0]),
        "g2_row": c(f(norm2_g)[0].reshape(1, D)),
        "gf": c(f(final_g).reshape(1, D)),
        "iota": np.tile(np.arange(NK, dtype=np.float32), (P, 1)),
    }
    outs = {
        "out_y": (T, D),
        "out_k": (T, AW),
        "out_v": (T, AW),
        "out_cp": (TAPS - 1, CH),
        "out_cs": (DEC_B, TAPS - 1, CH),
    }
    nc = bacc.Bacc("TRN2", target_bir_lowering=False, num_devices=1)
    d = Names()
    for name, a in given.items():
        d[name] = nc.dram_tensor(f"in_{name}", a.shape, F32, kind="ExternalInput").ap()
    for name, shape in outs.items():
        d[name] = nc.dram_tensor(name, shape, F32, kind="ExternalOutput").ap()
    d["x1"] = nc.dram_tensor("x1_kept", (T, D), F32, kind="Internal").ap()
    build(nc, d)
    r = run_bass_kernel_spmd(nc, [{f"in_{n}": a for n, a in given.items()}], core_ids=[0]).results[0]
    y, k, v = r["out_y"], r["out_k"], r["out_v"]
    heads = lambda a, b, t: a.reshape(1, b, t, NH, HD)
    return (y[:SEQ].reshape(1, SEQ, D), y[SEQ:].reshape(DEC_B, DEC_T, D),
            heads(k[:SEQ], 1, SEQ), heads(v[:SEQ], 1, SEQ), r["out_cp"].reshape(1, 1, TAPS - 1, CH),
            heads(k[SEQ:], DEC_B, DEC_T), heads(v[SEQ:], DEC_B, DEC_T),
            r["out_cs"].reshape(1, DEC_B, TAPS - 1, CH))
```
